# Optimizing a Trainium2 kernel written in Bass

```python
import jax, jax.numpy as jnp
from jax import lax
import numpy as np

D_MODEL = 1024
BATCH = 1
SEQ = 1024
DEPTH = 1

MEM_LEN = 256
D_MIX = D_MODEL
SB_HEAD_DIM = 64
SB_WIDTH = D_MIX // 2
SB_HEADS = SB_WIDTH // SB_HEAD_DIM
POOL_WIDTH = D_MIX - SB_WIDTH
POOL_WINDOWS = (2, 4, 8, 16)
POOL_GROUPS = len(POOL_WINDOWS)
POOL_GROUP_DIM = POOL_WIDTH // POOL_GROUPS
IN_COLS = 3 * SB_WIDTH + POOL_WIDTH
Q_BLOCK = 128
MEM_HEADS = 4
MEM_HEAD_DIM = D_MODEL // MEM_HEADS
D_FF = 256 * ((8 * D_MODEL // 3 + 255) // 256)
FFN_RESIDUAL_WEIGHT = 0.5
EPS = 1e-6

kernel_name = "hybrid_stickbreaking_pool_macaron_layer"

def rmsnorm(x, g):
    xf = x.astype(jnp.float32)
    xf = xf * lax.rsqrt(jnp.mean(xf * xf, axis=-1, keepdims=True) + EPS)
    return xf.astype(x.dtype) * g

def swiglu(h, w_gate, w_up, w_down):
    return (jax.nn.silu(h @ w_gate) * (h @ w_up)) @ w_down

def stick_breaking_attention(q, k, v):
    S = q.shape[2]
    scale = q.shape[-1] ** -0.5
    outs = []
    for i in range(S // Q_BLOCK):
        q0 = i * Q_BLOCK
        kv_len = q0 + Q_BLOCK
        q_blk = q[:, :, q0:kv_len]
        k_pre = k[:, :, :kv_len]
        v_pre = v[:, :, :kv_len]
        z = jnp.einsum("bhqd,bhkd->bhqk", q_blk, k_pre).astype(jnp.float32) * scale
        q_pos = q0 + jnp.arange(Q_BLOCK)
        k_pos = jnp.arange(kv_len)
        strict = k_pos[None, :] < q_pos[:, None]
        log_rest = jnp.where(strict, jax.nn.log_sigmoid(-z), 0.0)
        suffix = lax.cumsum(log_rest, axis=3, reverse=True) - log_rest
        a = jnp.where(strict, jnp.exp(jax.nn.log_sigmoid(z) + suffix), 0.0)
        outs.append(jnp.einsum("bhqk,bhkd->bhqd", a.astype(v.dtype), v_pre))
    return jnp.concatenate(outs, axis=2)

def causal_multiscale_pool(u):
    B, S, _ = u.shape
    uf = u.astype(jnp.float32).reshape(B, S, POOL_GROUPS, POOL_GROUP_DIM)
    cs = jnp.concatenate([jnp.zeros_like(uf[:, :1]), jnp.cumsum(uf, axis=1)], axis=1)
    pos = jnp.arange(S)
    pooled = []
    for g, w in enumerate(POOL_WINDOWS):
        hi = cs[:, 1:, g]
        lo = cs[:, jnp.maximum(pos + 1 - w, 0), g]
        count = jnp.minimum(pos + 1, w).astype(jnp.float32)
        pooled.append((hi - lo) / count[None, :, None])
    pooled = jnp.stack(pooled, axis=2)
    return (pooled - uf).astype(u.dtype)

def memory_cross_attention(h, mem_n, w_q, w_kv, w_o):
    B, S, _ = h.shape
    M = mem_n.shape[1]
    q = (h @ w_q).reshape(B, S, MEM_HEADS, MEM_HEAD_DIM)
    kv = (mem_n @ w_kv).reshape(B, M, 2, MEM_HEADS, MEM_HEAD_DIM)
    k, v = kv[:, :, 0], kv[:, :, 1]
    s = jnp.einsum("bshd,bmhd->bhsm", q, k).astype(jnp.float32) * (MEM_HEAD_DIM ** -0.5)
    p = jax.nn.softmax(s, axis=-1).astype(v.dtype)
    o = jnp.einsum("bhsm,bmhd->bshd", p, v).reshape(B, S, D_MODEL)
    return o @ w_o

def parallel_head_group_mixer(h, w_in, w_pool, pool_scale, w_out):
    B, S, _ = h.shape
    proj = h @ w_in
    q, k, v, u = jnp.split(proj, [SB_WIDTH, 2 * SB_WIDTH, 3 * SB_WIDTH], axis=-1)
    to_heads = lambda t: t.reshape(B, S, SB_HEADS, SB_HEAD_DIM).transpose(0, 2, 1, 3)
    o_sb = stick_breaking_attention(to_heads(q), to_heads(k), to_heads(v))
    o_sb = o_sb.transpose(0, 2, 1, 3).reshape(B, S, SB_WIDTH)
    pooled = causal_multiscale_pool(u)
    o_pool = jnp.einsum("bsgc,gcd->bsgd", pooled, w_pool).reshape(B, S, POOL_WIDTH) * pool_scale
    return jnp.concatenate([o_sb, o_pool], axis=-1) @ w_out

def setup_inputs(seed: int = 0) -> dict:
    key = jax.random.key(seed)
    ks = jax.random.split(key, 24)

    def dense(k, shape, fan_in):
        return jax.random.normal(k, shape, jnp.float32) * fan_in ** -0.5

    def gain(k, shape):
        return 1.0 + 0.02 * jax.random.normal(k, shape, jnp.float32)

    L, D = DEPTH, D_MODEL
    return {
        "x": jax.random.normal(ks[0], (BATCH, SEQ, D), jnp.float32),
        "mem": jax.random.normal(ks[1], (BATCH, MEM_LEN, D), jnp.float32),
        "ffn1_norm": gain(ks[2], (L, D)),
        "ffn1_w_gate": dense(ks[3], (L, D, D_FF), D),
        "ffn1_w_up": dense(ks[4], (L, D, D_FF), D),
        "ffn1_w_down": dense(ks[5], (L, D_FF, D), D_FF),
        "mix_norm": gain(ks[6], (L, D)),
        "w_in": dense(ks[7], (L, D, IN_COLS), D),
        "w_pool": dense(ks[8], (L, POOL_GROUPS, POOL_GROUP_DIM, POOL_GROUP_DIM), POOL_GROUP_DIM),
        "pool_scale": gain(ks[9], (L, POOL_WIDTH)),
        "w_out": dense(ks[10], (L, D_MIX, D), D_MIX),
        "mem_q_norm": gain(ks[11], (L, D)),
        "mem_kv_norm": gain(ks[12], (L, D)),
        "mem_w_q": dense(ks[13], (L, D, D), D),
        "mem_w_kv": dense(ks[14], (L, D, 2 * D), D),
        "mem_w_o": dense(ks[15], (L, D, D), D),
        "ffn2_norm": gain(ks[16], (L, D)),
        "ffn2_w_gate": dense(ks[17], (L, D, D_FF), D),
        "ffn2_w_up": dense(ks[18], (L, D, D_FF), D),
        "ffn2_w_down": dense(ks[19], (L, D_FF, D), D_FF),
        "final_norm": gain(ks[20], (D,)),
    }

def reference(x, mem, ffn1_norm, ffn1_w_gate, ffn1_w_up, ffn1_w_down, mix_norm, w_in, w_pool,
              pool_scale, w_out, mem_q_norm, mem_kv_norm, mem_w_q, mem_w_kv, mem_w_o,
              ffn2_norm, ffn2_w_gate, ffn2_w_up, ffn2_w_down, final_norm):
    for l in range(DEPTH):
        x = x + FFN_RESIDUAL_WEIGHT * swiglu(rmsnorm(x, ffn1_norm[l]), ffn1_w_gate[l], ffn1_w_up[l], ffn1_w_down[l])
        x = x + parallel_head_group_mixer(rmsnorm(x, mix_norm[l]), w_in[l], w_pool[l], pool_scale[l], w_out[l])
        x = x + memory_cross_attention(rmsnorm(x, mem_q_norm[l]), rmsnorm(mem, mem_kv_norm[l]),
                                       mem_w_q[l], mem_w_kv[l], mem_w_o[l])
        x = x + FFN_RESIDUAL_WEIGHT * swiglu(rmsnorm(x, ffn2_norm[l]), ffn2_w_gate[l], ffn2_w_up[l], ffn2_w_down[l])
    return rmsnorm(x, final_norm)


_drawn_inputs = setup_inputs


def setup_inputs(seed=0):
    import zlib

    import numpy as np

    out = dict(_drawn_inputs(seed))
    spreads = {}
    factors = {'ffn1_norm': 6.43,
     'mix_norm': 4.202,
     'pool_scale': 5.936,
     'mem_q_norm': 8.0,
     'mem_kv_norm': 8.0,
     'ffn2_norm': 22.798,
     'final_norm': 8.691}
    for name, (base, spread) in spreads.items():
        noise = np.random.default_rng([zlib.crc32(name.encode()), seed]).standard_normal(out[name].shape)
        drawn = base * np.exp(spread * noise) if base else spread * noise
        out[name] = __import__('jax').numpy.asarray(drawn.astype(out[name].dtype))
    for name, factor in factors.items():
        out[name] = (out[name] * factor).astype(out[name].dtype)
    return out
```

```python
from contextlib import ExitStack

import concourse.bass as bass
from concourse import mybir

ALU = mybir.AluOpType
ACT = mybir.ActivationFunctionType
F32 = mybir.dt.float32
F32R = mybir.dt.float32r
AX_X = mybir.AxisListType.X

P = 128
HALF = 512
EPS = 1e-6
POOL_WINDOWS = (2, 4, 8, 16)
PAD = max(POOL_WINDOWS)


def layer_program(nc, x, mem, ffn1_norm, ffn1_w_gate, ffn1_w_up, ffn1_w_down, mix_norm, w_in, w_pool,
                  pool_scale, w_out, mem_q_norm, mem_kv_norm, mem_w_q, mem_w_kv, mem_w_o,
                  ffn2_norm, ffn2_w_gate, ffn2_w_up, ffn2_w_down, final_norm, out):
    _, SEQ, D = x.shape
    MEM = mem.shape[1]
    F = ffn1_w_gate.shape[2]
    DC = D // P
    TC = SEQ // P
    HT = HALF // P
    FC = F // P
    GROUPS = FC // 2
    MC = MEM // P
    SBW = D // 2
    HEADS = SBW // 64
    SB_SCALE = 64 ** -0.5
    MHEADS = 4
    HD = D // MHEADS // P
    MEM_SCALE = (D // MHEADS) ** -0.5
    NG = len(POOL_WINDOWS)
    PAIR_ORDER = (0, 3, 1, 2)
    AT_BLOCKS = 12
    AT_FIRST = {0: 8, 3: 0, 1: 8, 2: 0}
    assert D == 1024 and SEQ == 2 * HALF and GROUPS % 2 == 1 and MC == 2

    ctx = ExitStack()
    with ctx:
        def sb(name, shape, dt=F32, into=ctx):
            return into.enter_context(nc.sbuf_tensor(name, shape, dt))

        def sem(name):
            return ctx.enter_context(nc.semaphore(name))

        def shared(name, kib, *sets):
            made = {}
            for tensors in sets:
                with ExitStack() as scope:
                    for n, shape, dt in tensors:
                        made[n] = sb(n, shape, dt, scope)
            sb(name, [P, kib * 256], F32)
            return made

        xT = sb("xT", [P, DC, SEQ])
        act_hi = sb("act_hi", [P, DC, SEQ], F32R)
        act_lo = sb("act_lo", [P, DC, SEQ], F32R)
        ident = sb("ident", [P, P])
        ones = sb("ones", [P, P])
        gain_rows = sb("gain_rows", [5 * DC + NG, P])
        gains = sb("gains", [P, 5 * DC + NG])
        recip_count = sb("recip_count", [P, PAD])
        sq = sb("sq", [P, 2, HALF])
        ssq = sb("ssq", [P, SEQ])
        xn_tmp = sb("xn_tmp", [P, 2, HALF])
        diag = sb("diag", [P, HALF])
        var = sb("var", [P, 8, HT])
        std = sb("std", [P, 8, HT])
        rstd = sb("rstd", [P, 8, 4, HT])
        G1, GM, GQ, GKV, G2, GP = (DC * i for i in range(6))

        ffn_set = ExitStack()
        ffn_bufs = {}
        for n, shape, dt in (
            ("silu", [P, 2, HALF], F32), ("h_sum", [P, 2, HALF], F32),
            ("gain_all", [P, D], F32), ("y_row", [P, 2, D], F32), ("y_sq", [P, D], F32),
            ("gate_hi", [P, DC, P], F32R), ("gate_lo", [P, DC, P], F32R),
            ("up_hi", [P, DC, P], F32R), ("up_lo", [P, DC, P], F32R),
            ("gate_raw", [P, DC, P], F32), ("up_raw", [P, DC, P], F32), ("down_raw", [P, D], F32),
            ("down_hi", [P, 2, D], F32R), ("down_lo", [P, 2, D], F32R),
        ):
            ffn_bufs[n] = sb(n, shape, dt, ffn_set)
        with ExitStack() as scope:
            x_rows = sb("x_rows", [P, TC, D], F32, scope)
        h_hi = sb("h_hi", [P, 4, SEQ], F32R, ffn_set)
        h_lo = sb("h_lo", [P, 4, SEQ], F32R, ffn_set)
        ffn_set.close()
        silu, h_sum, gain_all, y_row, y_sq = (ffn_bufs[n] for n in ("silu", "h_sum", "gain_all", "y_row", "y_sq"))
        gate_hi, gate_lo, up_hi, up_lo = (ffn_bufs[n] for n in ("gate_hi", "gate_lo", "up_hi", "up_lo"))
        gate_raw, up_raw, down_raw = (ffn_bufs[n] for n in ("gate_raw", "up_raw", "down_raw"))
        down_hi, down_lo = ffn_bufs["down_hi"], ffn_bufs["down_lo"]

        r1 = shared("region1", 24,
                    [("wa_hi", [P, 2, DC, P], F32R), ("wa_lo", [P, 2, DC, P], F32R),
                     ("wa_raw", [P, 2, DC, P], F32)],
                    [("q_stack", [P, 2, SEQ], F32R), ("k_hi2", [P, 2, SEQ], F32R),
                     ("k_lo2", [P, 2, SEQ], F32R)],
                    [("wb_hi", [P, 2, DC, P], F32R), ("wb_lo", [P, 2, DC, P], F32R),
                     ("wb_raw", [P, 2, DC, P], F32)])
        r2 = shared("region2", 32,
                    [("v_hi", [P, TC, SBW], F32R), ("v_lo", [P, TC, SBW], F32R)],
                    [("memT_hi", [P, DC, MEM], F32R), ("memT_lo", [P, DC, MEM], F32R),
                     ("mem_rows", [P, MC, D], F32), ("mem_tmp", [P, 2, MEM], F32),
                     ("mem_sq", [P, D], F32)],
                    [("mq_hi", [P, DC, HALF], F32R), ("mq_lo", [P, DC, HALF], F32R)])
        r3 = shared("region3", 16,
                    [("pooled", [P, NG, SEQ], F32)],
                    [("beta", [P, 4, SEQ], F32)],
                    [("mk_hi", [P, DC, MEM], F32R), ("mk_lo", [P, DC, MEM], F32R)])
        r4 = shared("region4", 36,
                    [("u", [P, PAD + SEQ], F32), ("s0", [P, PAD + SEQ], F32), ("s1", [P, PAD + SEQ], F32),
                     ("pool_hi", [P, 2, HALF], F32R), ("pool_lo", [P, 2, HALF], F32R),
                     ("wp_raw", [P, NG, P], F32), ("wp_hi", [P, NG, P], F32R), ("wp_lo", [P, NG, P], F32R),
                     ("stage_hi", [P, 2, HALF], F32R), ("stage_lo", [P, 2, HALF], F32R),
                     ("head_mean", [P, PAD], F32)],
                    [("rest", [P, 3, SEQ], F32),
                     ("aT_hi", [P, AT_BLOCKS, 2 * P], F32R), ("aT_lo", [P, AT_BLOCKS, 2 * P], F32R)],
                    [("mv_hi", [P, MC, D], F32R), ("mv_lo", [P, MC, D], F32R),
                     ("prob", [P, 2, HT, MEM], F32),
                     ("pT_hi", [P, MC, HALF], F32R), ("pT_lo", [P, MC, HALF], F32R)])
        wa_hi, wa_lo, wa_raw = r1["wa_hi"], r1["wa_lo"], r1["wa_raw"]
        wb_hi, wb_lo, wb_raw = r1["wb_hi"], r1["wb_lo"], r1["wb_raw"]
        q_stack, k_hi2, k_lo2 = r1["q_stack"], r1["k_hi2"], r1["k_lo2"]
        v_hi, v_lo = r2["v_hi"], r2["v_lo"]
        memT_hi, memT_lo, mem_rows, mem_tmp, mem_sq = (
            r2["memT_hi"], r2["memT_lo"], r2["mem_rows"], r2["mem_tmp"], r2["mem_sq"])
        mq_hi, mq_lo = r2["mq_hi"], r2["mq_lo"]
        pooled, mk_hi, mk_lo = r3["pooled"], r3["mk_hi"], r3["mk_lo"]
        u, s0, s1, head_mean = r4["u"], r4["s0"], r4["s1"], r4["head_mean"]
        pool_hi, pool_lo = r4["pool_hi"], r4["pool_lo"]
        wp_raw, wp_hi, wp_lo = r4["wp_raw"], r4["wp_hi"], r4["wp_lo"]
        stage_hi, stage_lo = r4["stage_hi"], r4["stage_lo"]
        beta, rest, aT_hi, aT_lo = r3["beta"], r4["rest"], r4["aT_hi"], r4["aT_lo"]
        mv_hi, mv_lo, prob, pT_hi, pT_lo = r4["mv_hi"], r4["mv_lo"], r4["prob"], r4["pT_hi"], r4["pT_lo"]
        mstat = sb("mstat", [P, 2, 4, HT])
        mvar = sb("mvar", [P, 8, MC])
        fstat = sb("fstat", [P, 8, TC])

        q_spill_hi = nc.dram_tensor("q_spill_hi", [SBW, SEQ], F32).ap()
        q_spill_lo = nc.dram_tensor("q_spill_lo", [SBW, SEQ], F32).ap()
        k_spill_hi = nc.dram_tensor("k_spill_hi", [SBW, SEQ], F32).ap()
        k_spill_lo = nc.dram_tensor("k_spill_lo", [SBW, SEQ], F32).ap()

        ps = ctx.enter_context(nc.psum_tensor("ps", [P, 8, HALF], F32))

        s_const, s_counts = sem("s_const"), sem("s_counts")
        s_rows_in = sem("s_rows_in")
        s_gains_ps, s_gains = sem("s_gains_ps"), sem("s_gains")
        s_x_in = [sem("s_x_in0"), sem("s_x_in1")]
        s_xt_ps, s_xt = sem("s_xt_ps"), sem("s_xt")
        s_sq, s_ssq, s_tot, s_var, s_std = sem("s_sq"), sem("s_ssq"), sem("s_tot"), sem("s_var"), sem("s_std")
        s_chain, s_diag, s_bc = sem("s_chain"), sem("s_diag"), sem("s_bc")
        s_xn_tmp, s_xn_hi, s_xn = sem("s_xn_tmp"), sem("s_xn_hi"), sem("s_xn")

        class Ffn:
            def __init__(self, tag, gate, up, down, norm):
                self.gate, self.up, self.down = gate[0], up[0], down[0]
                self.norm = norm
                (self.gate_in, self.up_in, self.down_in,
                 self.gate_hi, self.gate_lo, self.up_hi, self.up_lo,
                 self.down_hi, self.down_lo,
                 self.gate_done, self.up_done,
                 self.silu, self.prod, self.h_hi, self.h_lo,
                 self.out_done, self.out_free) = (
                    sem(f"{tag}_{n}") for n in (
                        "gate_in", "up_in", "down_in", "gate_hi", "gate_lo", "up_hi", "up_lo", "down_hi",
                        "down_lo", "gate_done", "up_done", "silu", "prod", "h_hi", "h_lo",
                        "out_done", "out_free"))

        f1 = Ffn("f1", ffn1_w_gate, ffn1_w_up, ffn1_w_down, 0)
        f2 = Ffn("f2", ffn2_w_gate, ffn2_w_up, ffn2_w_down, 6)
        BANKS = 4
        LAST = 2 * DC * (GROUPS - 1)

        a_in = [sem("a_in0"), sem("a_in1")]
        a_hi, a_lo = sem("a_hi"), sem("a_lo")
        a_out, a_ehi, a_free = sem("a_out"), sem("a_ehi"), sem("a_free")
        s_wsum, s_pooled, s_pads, s_pchain, s_dchain = (
            sem("s_wsum"), sem("s_pooled"), sem("s_pads"), sem("s_pchain"), sem("s_dchain"))
        s_wp_in, s_wp_hi, s_wp = sem("s_wp_in"), sem("s_wp_hi"), sem("s_wp")
        s_pl_hi, s_pl = sem("s_pl_hi"), sem("s_pl")
        s_spill = [sem("s_spill0"), sem("s_spill1")]
        s_stack = [sem("s_stack0"), sem("s_stack1")]
        s_z, s_sig, s_mask, s_scan = sem("s_z"), sem("s_sig"), sem("s_mask"), sem("s_scan")
        s_a, s_a_far = sem("s_a"), sem("s_a_far")
        s_aT_ps, s_aT_hi, s_aT = sem("s_aT_ps"), sem("s_aT_hi"), sem("s_aT")
        s_o, s_o_hi, s_o_free = sem("s_o"), sem("s_o_hi"), sem("s_o_free")

        b_in = [sem("b_in0"), sem("b_in1")]
        b_hi, b_lo = sem("b_hi"), sem("b_lo")
        b_out, b_ehi, b_free = sem("b_out"), sem("b_ehi"), sem("b_free")
        s_mem_in, s_mem_sq, s_mem_chain, s_mem_scaled = (
            sem("s_mem_in"), sem("s_mem_sq"), sem("s_mem_chain"), sem("s_mem_scaled"))
        s_memT_ps, s_memT_tmp, s_memT_hi, s_memT = (
            sem("s_memT_ps"), sem("s_memT_tmp"), sem("s_memT_hi"), sem("s_memT"))
        s_S, s_mx, s_nmx, s_exp, s_rinv, s_prob = (
            sem("s_S"), sem("s_mx"), sem("s_nmx"), sem("s_exp"), sem("s_rinv"), sem("s_prob"))
        s_pT_ps, s_pT_hi, s_pT = sem("s_pT_ps"), sem("s_pT_hi"), sem("s_pT")
        s_fin_in, s_yT, s_ysq, s_fchain, s_fstd, s_y = (
            sem("s_fin_in"), sem("s_yT"), sem("s_ysq"), sem("s_fchain"), sem("s_fstd"), sem("s_y"))
        s_out = [sem("s_out0"), sem("s_out1")]

        def tok(half):
            return slice(half * HALF, (half + 1) * HALF)

        def cols(w, n):
            return w[:, n * P:(n + 1) * P].rearrange("(c p) m -> p c m", p=P)

        def plain(ap):
            return ap.bitcast(F32)

        wi = w_in[0]
        A_TILES = ([("u", g, cols(wi, 3 * SBW // P + g)) for g in range(NG)]
                   + [("v", j, cols(wi, 2 * SBW // P + j)) for j in range(SBW // P)]
                   + [(kind, j, cols(wi, (0 if kind == "q" else SBW // P) + j))
                      for j in range(SBW // P) for kind in ("q", "k")])
        A_UNITS, a_through = [], []
        for n, (kind, j, _) in enumerate(A_TILES):
            if kind != "v":
                A_UNITS += [(n, kind, j, half) for half in range(2)]
            elif j % 2:
                A_UNITS += [(n, "v", j // 2, t) for t in range(TC)]
            a_through.append(len(A_UNITS) + (TC if kind == "v" and j % 2 == 0 else 0))
        A_PROJ, A_U = len(A_UNITS), 2 * NG
        A_UNITS += [(None, "pool", g, half) for g in range(NG) for half in range(2)]

        mk_w, mv_w = mem_w_kv[0][:, 0:D], mem_w_kv[0][:, D:2 * D]
        B_TILES = [(kind, j, cols(w, j)) for kind, w in (
            ("out", w_out[0]), ("mk", mk_w), ("mv", mv_w), ("q0", mem_w_q[0]), ("q1", mem_w_q[0]),
            ("o0", mem_w_o[0]), ("o1", mem_w_o[0])) for j in range(DC)]
        B0 = {kind: DC * i for i, kind in enumerate(("out", "mk", "mv", "q0", "q1", "o0", "o1"))}

        def tiles(kind, lo, hi):
            return [("tile", B0[kind] + j) for j in range(lo, hi)]

        def xn_steps(q, lo, hi):
            return [("xn", q, c) for c in range(lo, hi)]

        B_STEPS = tiles("out", 0, 1) + [("mem_rms",)] + tiles("out", 1, 3) + [("memT",)] + tiles("out", 3, DC)
        B_STEPS += [("tot", 4)] + tiles("mk", 0, 1) + [("tot", 5), ("bc", 4)] + tiles("mk", 1, 2) + [("bc", 5)]
        B_STEPS += xn_steps(4, 0, 2) + tiles("mk", 2, 3) + xn_steps(4, 2, 4) + tiles("mk", 3, 4)
        B_STEPS += xn_steps(4, 4, 6) + tiles("mk", 4, 5) + xn_steps(4, 6, 8) + tiles("mk", 5, 6)
        B_STEPS += xn_steps(5, 0, 2) + tiles("mk", 6, 7) + xn_steps(5, 2, 4) + tiles("mk", 7, 8)
        B_STEPS += xn_steps(5, 4, 8) + tiles("mv", 0, DC) + tiles("q0", 0, DC)
        for h in range(MHEADS):
            B_STEPS += [("S", 0, h)] + tiles("q1", HD * h, HD * h + 1) + [("T", 0, h)]
            B_STEPS += tiles("q1", HD * h + 1, HD * (h + 1)) + [("PV", 0, h)]
        for h in range(MHEADS):
            B_STEPS += [("S", 1, h)] + tiles("o0", HD * h, HD * h + 1) + [("T", 1, h)]
            B_STEPS += tiles("o0", HD * h + 1, HD * (h + 1)) + [("PV", 1, h)]
        B_STEPS += tiles("o1", 0, 1) + [("tot", 6)] + tiles("o1", 1, 2) + [("bc", 6)]
        for j in range(2, DC - 2):
            B_STEPS += xn_steps(6, 2 * j - 4, 2 * j - 2) + tiles("o1", j, j + 1)
        B_STEPS += tiles("o1", DC - 2, DC)
        b_first, b_hi_of, n_units, n_hi, b_through = {}, {}, 0, 0, [0] * len(B_TILES)
        for step in B_STEPS:
            b_first[step] = n_units
            kind = B_TILES[step[1]][0] if step[0] == "tile" else None
            made = HD if step[0] == "PV" else 0
            if kind:
                made = {"out": 2, "mv": MC * (step[1] % 2)}.get(kind, 1)
            for k in range(n_units, n_units + made):
                b_hi_of[k] = n_hi
                n_hi += kind not in ("out", "o0", "o1")
            n_units += made
            if kind:
                b_through[step[1]] = n_units + (MC if kind == "mv" and step[1] % 2 == 0 else 0)
        ADDS = ("out", "o0", "o1")

        def add_halves(kind):
            return (0, 1) if kind == "out" else (int(kind[1]),)

        def pv_step(w):
            return ("PV", w // MHEADS, w % MHEADS)

        def tail_steps(q):
            steps = []
            for k in range(2 * DC):
                steps.append(("add", k))
                if k == DC + 1:
                    steps.append(("tot", q))
                if k == DC + 3:
                    steps.append(("bc", q))
                if k >= DC + 4:
                    steps.append(("xn", q, k - DC - 4))
            return steps + [("xn", q, c) for c in (4, 5)] + [("tot", q + 1)] + [("xn", q, c) for c in (6, 7)]

        M = HEADS * TC
        W = M // 2
        turns_before = [0]
        for m in range(M):
            i = 2 * PAIR_ORDER[m % TC // 2] + m % 2
            turns_before.append(turns_before[-1] + i // 4 + 1)

        def tile_at(m):
            return m // TC, 2 * PAIR_ORDER[m % TC // 2] + m % 2

        def pair_at(w):
            return w // (TC // 2), PAIR_ORDER[w % (TC // 2)]

        z_bank, z_free_after, holds = [], [], {}
        for m in range(M):
            i, first = tile_at(m)[1], (z_bank[-1][1] % 4 if m else 0)
            z_bank.append((first, first + i // 4 + 1))
            z_free_after.append(max([holds.get(b, -1) + 1 for b in range(*z_bank[m])]))
            holds.update((b, m) for b in range(*z_bank[m]))
        assert all(end <= 4 for _, end in z_bank)

        def weighed(m):
            return sum(tile_at(k)[1] >= 4 for k in range(m + 1))

        def turns(m):
            i = tile_at(m)[1]
            return [(turns_before[m] + n, 4 + (turns_before[m] + n) % 3, 4 * n, min(4 * n + 4, i + 1))
                    for n in range(i // 4 + 1)]

        def aT_part(buf, m, lo_, hi_):
            first = AT_FIRST[tile_at(m)[1] // 2]
            return buf[:, first + lo_:first + hi_, (m % 2) * P:(m % 2 + 1) * P]
        STICK_LAG, TURN_LAG, VALUE_LAG = 1, 3, 6

        block = ctx.enter_context(nc.Block())

        @block.sync
        def _(sp):
            for i, w in enumerate((ffn1_norm, mix_norm, mem_q_norm, mem_kv_norm, ffn2_norm)):
                sp.dma_start(gain_rows[DC * i:DC * (i + 1), :],
                             w.rearrange("a (c p) -> (a c) p", p=P)).then_inc(s_rows_in, 16)
            sp.dma_start(gain_rows[GP:GP + NG, :],
                         pool_scale.rearrange("a (c p) -> (a c) p", p=P)).then_inc(s_rows_in, 16)
            for t in range(TC):
                sp.dma_start(x_rows[:, t, :], x[0, t * P:(t + 1) * P, :]).then_inc(s_x_in[t // HT], 16)

            def ffn_loads(F_):
                def gate_up(c, first=False):
                    if not first:
                        sp.wait_ge(F_.gate_lo, c)
                    sp.dma_start(gate_raw[:], F_.gate[:, bass.ds(c * P, P)]
                                 .rearrange("(c p) m -> p c m", p=P)).then_inc(F_.gate_in, 16)
                    if not first:
                        sp.wait_ge(F_.up_lo, c)
                    sp.dma_start(up_raw[:], F_.up[:, bass.ds(c * P, P)]
                                 .rearrange("(c p) m -> p c m", p=P)).then_inc(F_.up_in, 16)

                def down(c, first=False):
                    if not first:
                        sp.wait_ge(F_.down_lo, c)
                    sp.dma_start(down_raw[:], F_.down[bass.ds(c * P, P), :]).then_inc(F_.down_in, 16)

                gate_up(0, first=True)
                gate_up(1)
                gate_up(2)
                down(0, first=True)
                with sp.Fori(0, FC - 3) as it:
                    gate_up(it + 3)
                    down(it + 1)
                sp.wait_ge(F_.gate_lo, FC)
                sp.dma_start(gate_raw[:].rearrange("p c m -> p (c m)"),
                             F_.down[(FC - 2) * P:(FC - 1) * P, :]).then_inc(F_.gate_in, 16)
                sp.wait_ge(F_.up_lo, FC)
                sp.dma_start(up_raw[:].rearrange("p c m -> p (c m)"),
                             F_.down[(FC - 1) * P:, :]).then_inc(F_.up_in, 16)

            ffn_loads(f1)

            sp.wait_ge(f1.h_lo, 2 * FC)
            spilled = 0
            for n in range(len(A_TILES) + 1):
                if n < len(A_TILES):
                    if n >= 2:
                        sp.wait_ge(a_lo, n - 1)
                    sp.dma_start(wa_raw[:, n % 2], A_TILES[n][2]).then_inc(a_in[n % 2], 16)
                if n == 2:
                    sp.wait_ge(f1.out_done, 2 * DC * GROUPS)
                    sp.dma_start(wp_raw[:], w_pool[0].rearrange("g p m -> p g m")).then_inc(s_wp_in, 16)
                for k, (nn, kind, j, half) in enumerate(A_UNITS):
                    if nn == n - 1 and kind in ("q", "k"):
                        to_hi, to_lo = (q_spill_hi, q_spill_lo) if kind == "q" else (k_spill_hi, k_spill_lo)
                        sp.wait_ge(a_free, k + 1)
                        sp.dma_start(to_hi[j * P:(j + 1) * P, tok(half)],
                                     plain(stage_hi[:, half])).then_inc(s_spill[half], 16)
                        sp.dma_start(to_lo[j * P:(j + 1) * P, tok(half)],
                                     plain(stage_lo[:, half])).then_inc(s_spill[half], 16)
                        spilled += 1
            for half in range(2):
                sp.wait_ge(s_spill[half], 32 * (spilled // 2))
            sp.wait_ge(a_out, A_PROJ)
            for h in range(HEADS):
                if h >= 2:
                    sp.wait_ge(s_z, TC * (h - 1))
                rows = slice(64 * h, 64 * (h + 1))
                for to, lower, upper in ((q_stack, q_spill_hi, q_spill_lo), (k_hi2, k_spill_hi, k_spill_hi),
                                         (k_lo2, k_spill_lo, k_spill_lo)):
                    sp.dma_start(plain(to[0:64, h % 2]), lower[rows, :]).then_inc(s_stack[h % 2], 16)
                    sp.dma_start(plain(to[64:P, h % 2]), upper[rows, :]).then_inc(s_stack[h % 2], 16)

            sp.wait_ge(s_z, M)
            for n, (_, _, src) in enumerate(B_TILES):
                if n >= 2:
                    sp.wait_ge(b_lo, n - 1)
                sp.dma_start(wb_raw[:, n % 2], src).then_inc(b_in[n % 2], 16)
                if n == 1:
                    sp.wait_ge(s_o, W)
                    for c in range(MC):
                        sp.dma_start(mem_rows[:, c, :], mem[0, c * P:(c + 1) * P, :]).then_inc(s_mem_in, 16)

            sp.wait_ge(s_S, 2 * MHEADS)
            sp.wait_ge(b_free, b_first[pv_step(2 * MHEADS - 1)] + HD)
            ffn_loads(f2)
            sp.wait_ge(b_out, n_units)
            sp.dma_start(gain_all[:], final_norm.rearrange("(a d) -> a d", a=1)
                         .broadcast_to([P, D])).then_inc(s_fin_in, 16)
            for t in range(TC):
                sp.wait_ge(s_y, t + 1)
                sp.dma_start(out[0, t * P:(t + 1) * P, :], y_row[:, t % 2, :]).then_inc(s_out[t % 2], 16)
            for slot in range(2):
                sp.wait_ge(s_out[slot], 16 * TC // 2)

        @block.gpsimd
        def _(pool):
            pool.memset(ident[:], 0.0).then_inc(s_const, 1)
            pool.wait_ge(s_const, 1)
            pool.affine_select(out=ident[:], in_=ident[:], compare_op=ALU.not_equal, fill=1.0, base=0,
                               pattern=[[-1, P]], channel_multiplier=1).then_inc(s_const, 1)
            pool.memset(ones[:], 1.0).then_inc(s_const, 1)
            for t in range(PAD):
                pool.memset(recip_count[:, t:t + 1], 1.0 / (t + 1)).then_inc(s_counts, 1)

            def sum_squares(q, c, nth=None):
                nth = DC * q + c if nth is None else nth
                pool.wait_ge(s_sq, nth + 1)
                if c == 0:
                    if q >= 2:
                        pool.wait_ge(s_tot, q - 1)
                    pool.tensor_copy(ssq[:, tok(q % 2)], sq[:, nth % 2]).then_inc(s_ssq, 1)
                else:
                    pool.wait_ge(s_ssq, nth)
                    pool.tensor_tensor(ssq[:, tok(q % 2)], ssq[:, tok(q % 2)], sq[:, nth % 2],
                                       ALU.add).then_inc(s_ssq, 1)

            for q in range(4):
                for c in range(DC):
                    sum_squares(q, c)

            pool.wait_ge(f1.out_done, 2 * DC * GROUPS)
            for buf in (u, s0, s1):
                pool.memset(buf[:, 0:PAD], 0.0).then_inc(s_pads, 1)
            pool.wait_ge(s_pads, 3)
            links = 0
            for g, w in enumerate(POOL_WINDOWS):
                pool.wait_ge(a_free, 2 * (g + 1))
                if g:
                    pool.wait_ge(s_pooled, g)
                src, step, k = u, 1, 0
                while step < w:
                    dst = (s0, s1)[k % 2]
                    ins = pool.tensor_tensor(dst[:, PAD:], src[:, PAD:], src[:, PAD - step:PAD + SEQ - step],
                                             ALU.add)
                    step, src, k = 2 * step, dst, k + 1
                    if step < w:
                        links += 1
                        ins.then_inc(s_pchain, 1)
                        pool.wait_ge(s_pchain, links)
                    else:
                        ins.then_inc(s_wsum, 1)

            def mask(m):
                i = tile_at(m)[1]
                for nth, (buf, slot, fill) in enumerate(((rest, m % 3, 1.0), (beta, m % 4, 0.0))):
                    diagonal = buf[:, slot, i * P:(i + 1) * P]
                    pool.wait_ge(s_sig, 2 * m + nth + 1)
                    pool.affine_select(out=diagonal, in_=diagonal,
                                       compare_op=ALU.is_gt, fill=fill, base=0, pattern=[[-1, P]],
                                       channel_multiplier=1).then_inc(s_mask, 1)

            def weigh(m):
                n = min((tile_at(m)[1] + 1) * P, HALF + 1)
                pool.wait_ge(s_mask, 2 * (m + 1))
                pool.wait_ge(s_scan, m + 1)
                pool.tensor_tensor(beta[:, m % 4, 0:n - 1], beta[:, m % 4, 0:n - 1], rest[:, m % 3, 1:n],
                                   ALU.mult).then_inc(s_a, 1)

            for s in range(M + 1):
                if s < M:
                    mask(s)
                if s >= 1:
                    weigh(s - 1)

            for c in range(DC):
                for q in (4, 5):
                    sum_squares(q, c, nth=DC * 4 + 2 * c + q - 4)
            for q in (6, 7):
                for c in range(DC):
                    sum_squares(q, c)

        @block.tensor
        def _(pe):
            def three(to, w_hi, w_lo, m_hi, m_lo, first, last):
                pe.matmul(to, w_lo, m_hi, start=first, stop=False)
                pe.matmul(to, w_hi, m_lo, start=False, stop=False)
                return pe.matmul(to, w_hi, m_hi, start=False, stop=last)

            def norm_tot(q):
                pe.wait_ge(s_ssq, DC * (q + 1) if q != 4 else DC * 6 - 1)
                half = q % 2
                for j in range(HT):
                    mm = pe.matmul(ps[:, half, 2 * j:2 * j + 2],
                                   ssq[:, half * HALF + j * P:half * HALF + (j + 1) * P],
                                   ones[:, 0:2], start=True, stop=True)
                mm.then_inc(s_tot, 1)

            def norm_bc(q):
                pe.wait_ge(s_diag, q + 1)
                pe.matmul(ps[:, 2 + q % 2, :], ones[:], diag[:], start=True, stop=True).then_inc(s_bc, 1)

            pe.wait_ge(s_const, 3)
            pe.wait_ge(s_rows_in, 16 * 6)
            rows = GP + NG
            pe.transpose(ps[:, 0, 0:rows], gain_rows[:], ident[0:rows, 0:rows]).then_inc(s_gains_ps, 1)
            for k in range(2 * DC):
                half, c = divmod(k, DC)
                if c == 0:
                    pe.wait_ge(s_x_in[half], 16 * HT)
                if k >= 4:
                    pe.wait_ge(s_xt, k - 3)
                for t in range(HT):
                    mm = pe.transpose(ps[:, 4 + k % 4, t * P:(t + 1) * P],
                                      x_rows[:, half * HT + t, c * P:(c + 1) * P], ident[:])
                mm.then_inc(s_xt_ps, 1)
            pe.wait_ge(s_gains, 1)
            norm_tot(0)
            norm_bc(0)
            norm_tot(1)

            def ffn(F_, final):
                def product(c, which, half, first=False, xn=False):
                    whi, wlo, ready, done, busy = (
                        (gate_hi, gate_lo, F_.gate_lo, F_.gate_done, F_.silu),
                        (up_hi, up_lo, F_.up_lo, F_.up_done, F_.prod))[which]
                    pe.wait_ge(ready, c + 1)
                    if not first:
                        pe.wait_ge(busy, 2 * c - 1 + half)
                    for d in range(DC):
                        if xn:
                            pe.wait_ge(s_xn, DC * (F_.norm + half) + d + 1)
                        mm = three(ps[:, 2 * which + half, :], whi[:, d, :], wlo[:, d, :],
                                   act_hi[:, d, tok(half)], act_lo[:, d, tok(half)], d == 0, d == DC - 1)
                    mm.then_inc(done, 1)

                def gate_up(c):
                    for which in range(2):
                        for half in range(2):
                            product(c, which, half)

                def down(g, parity):
                    pe.wait_ge(F_.down_lo, 2 * g + 2)
                    pe.wait_ge(F_.h_lo, 4 * g + 4)
                    for k in range(2 * DC):
                        half, d = divmod(k, DC)
                        pe.wait_ge(F_.out_free, 2 * DC * g + k + 1)
                        for s in range(2):
                            blk = slice(d * P, (d + 1) * P)
                            mm = three(ps[:, 4 + k % 4, :], down_hi[:, s, blk], down_lo[:, s, blk],
                                       h_hi[:, 2 * parity + s, tok(half)], h_lo[:, 2 * parity + s, tok(half)],
                                       s == 0, s == 1)
                        mm.then_inc(F_.out_done, 1)

                product(0, 0, 0, first=True, xn=True)
                product(0, 1, 0, first=True)
                norm_bc(F_.norm + 1)
                product(0, 0, 1, first=True, xn=True)
                product(0, 1, 1, first=True)
                gate_up(1)
                with pe.Fori(0, (GROUPS - 1) // 2) as it:
                    for parity in (1, 0):
                        g = 2 * it + (1 if parity else 2)
                        gate_up(2 * g)
                        gate_up(2 * g + 1)
                        down(g - 1, 1 - parity)

                pe.wait_ge(F_.gate_lo, FC + 1)
                pe.wait_ge(F_.up_lo, FC + 1)
                pe.wait_ge(F_.h_lo, 2 * FC)

                def output(k):
                    half, d = divmod(k, DC)
                    pe.wait_ge(F_.out_free, LAST + k + 1)
                    for s, (whi, wlo) in enumerate(((gate_hi, gate_lo), (up_hi, up_lo))):
                        mm = three(ps[:, 4 + k % 4, :], whi[:, d, :], wlo[:, d, :],
                                   h_hi[:, s, tok(half)], h_lo[:, s, tok(half)], s == 0, s == 1)
                    mm.then_inc(F_.out_done, 1)

                if final:
                    for k in range(2 * DC):
                        output(k)
                        if k >= DC + 1 and k % 2:
                            y_turn((k - DC) // 2)
                    for t in range(HT, TC):
                        y_turn(t)
                else:
                    for step in tail_steps(2):
                        if step[0] == "add":
                            output(step[1])
                        elif step[0] == "tot":
                            norm_tot(step[1])
                        elif step[0] == "bc":
                            norm_bc(step[1])

            def y_turn(t):
                pe.wait_ge(f2.out_free, BANKS + LAST + DC * (t // HT + 1))
                if t >= 2:
                    pe.wait_ge(s_y, t - 1)
                for c in range(DC):
                    mm = pe.transpose(ps[:, 2 * (t % 2) + c // 4, (c % 4) * P:(c % 4 + 1) * P],
                                      xT[:, c, t * P:(t + 1) * P], ident[:])
                mm.then_inc(s_yT, 1)

            ffn(f1, final=False)

            for k, (n, kind, j, part) in enumerate(A_UNITS[:A_PROJ]):
                pe.wait_ge(a_lo, n + 1)
                if k >= 4:
                    pe.wait_ge(a_free, k - 3)
                if k == 1:
                    norm_bc(3)
                for d in range(DC):
                    if n == 0:
                        pe.wait_ge(s_xn, DC * (2 + part) + d + 1)
                    if kind == "v":
                        tt = slice(part * P, (part + 1) * P)
                        mm = three(ps[:, 4 + k % 4, 0:2 * P], act_hi[:, d, tt], act_lo[:, d, tt],
                                   wa_hi[:, :, d, :], wa_lo[:, :, d, :], d == 0, d == DC - 1)
                    else:
                        mm = three(ps[:, 4 + k % 4, :], wa_hi[:, n % 2, d, :], wa_lo[:, n % 2, d, :],
                                   act_hi[:, d, tok(part)], act_lo[:, d, tok(part)], d == 0, d == DC - 1)
                mm.then_inc(a_out, 1)
            pe.wait_ge(s_wp, 1)
            for k in range(A_PROJ, len(A_UNITS)):
                _, _, g, half = A_UNITS[k]
                pe.wait_ge(a_free, k - 3)
                pe.wait_ge(s_pl, k - A_PROJ + 1)
                three(ps[:, 4 + k % 4, :], wp_hi[:, g, :], wp_lo[:, g, :],
                      pool_hi[:, half], pool_lo[:, half], True, True).then_inc(a_out, 1)

            def scores(m):
                h, i = tile_at(m)
                if m % TC == 0:
                    pe.wait_ge(s_stack[h % 2], 96 * (h // 2 + 1))
                if z_free_after[m]:
                    pe.wait_ge(s_sig, 2 * z_free_after[m])
                n = (i + 1) * P
                for lo in range(0, n, HALF):
                    keys = slice(lo, min(n, lo + HALF))
                    z = ps[:, z_bank[m][0] + lo // HALF, 0:keys.stop - lo]
                    pe.matmul(z, q_stack[:, h % 2, i * P:(i + 1) * P], k_lo2[:, h % 2, keys],
                              start=True, stop=False)
                    mm = pe.matmul(z, q_stack[:, h % 2, i * P:(i + 1) * P], k_hi2[:, h % 2, keys],
                                   start=False, stop=True)
                mm.then_inc(s_z, 1)

            def turn(m):
                pe.wait_ge(s_a, m + 1)
                if weighed(m):
                    pe.wait_ge(s_a_far, weighed(m))
                for nth, bank, first, end in turns(m):
                    if nth >= 3:
                        pe.wait_ge(s_aT, nth - 2)
                    for j in range(first, end):
                        mm = pe.transpose(ps[:, bank, (j - first) * P:(j - first + 1) * P],
                                          beta[:, m % 4, j * P:(j + 1) * P], ident[:])
                    mm.then_inc(s_aT_ps, 1)

            def values(w):
                h, b = pair_at(w)
                pe.wait_ge(s_aT, turns_before[2 * w + 2])
                if w:
                    pe.wait_ge(s_o_free, w)
                pair = slice((h // 2) * P, (h // 2 + 1) * P)
                o = ps[:, 7, (w % 2) * 2 * P:(w % 2 + 1) * 2 * P]
                for j in range(2 * b + 2):
                    lo = P if j == 2 * b + 1 else 0
                    block = AT_FIRST[b] + j
                    mm = three(o[:, lo:], v_hi[:, j, pair], v_lo[:, j, pair],
                               aT_hi[:, block, lo:], aT_lo[:, block, lo:], j == 0, j == 2 * b + 1)
                mm.then_inc(s_o, 1)

            pe.wait_ge(a_free, len(A_UNITS))
            for s in range(M + VALUE_LAG):
                if s < M:
                    scores(s)
                if 0 <= s - TURN_LAG < M:
                    turn(s - TURN_LAG)
                if s >= VALUE_LAG and (s - VALUE_LAG) % 2 == 0:
                    values((s - VALUE_LAG) // 2)

            pe.wait_ge(s_o_free, W)
            for step in B_STEPS:
                k = b_first[step]
                if step[0] == "tile":
                    n = step[1]
                    kind, j, _ = B_TILES[n]
                    if kind == "mv" and j % 2 == 0:
                        continue
                    pe.wait_ge(b_lo, n + 1)
                    if kind == "mk" and j == 0:
                        pe.wait_ge(s_memT, DC)
                    if kind == "o0" and j == 0:
                        pe.wait_ge(b_free, b_first[pv_step(MHEADS - 1)] + HD)
                    if kind == "o1" and j == 0:
                        pe.wait_ge(b_free, b_first[pv_step(2 * MHEADS - 1)] + HD)
                    parts = {"out": (0, 1), "mk": (0,), "mv": (0, 1)}.get(kind) or (int(kind[1]),)
                    for part in parts:
                        if k >= 4:
                            pe.wait_ge(b_free, k - 3)
                        bank = ps[:, 4 + k % 4, :]
                        for d in range(DC):
                            ends = d == 0, d == DC - 1
                            if kind in ("q0", "q1") and j == 0:
                                pe.wait_ge(s_xn, DC * (4 + part) + d + 1)
                            if kind == "mk":
                                mm = three(bank[:, 0:MEM], wb_hi[:, n % 2, d, :], wb_lo[:, n % 2, d, :],
                                           memT_hi[:, d, :], memT_lo[:, d, :], *ends)
                            elif kind == "mv":
                                tt = slice(part * P, (part + 1) * P)
                                mm = three(bank[:, 0:2 * P], memT_hi[:, d, tt], memT_lo[:, d, tt],
                                           wb_hi[:, :, d, :], wb_lo[:, :, d, :], *ends)
                            else:
                                mm = three(bank, wb_hi[:, n % 2, d, :], wb_lo[:, n % 2, d, :],
                                           act_hi[:, d, tok(part)], act_lo[:, d, tok(part)], *ends)
                        mm.then_inc(b_out, 1)
                        k += 1
                elif step[0] == "memT":
                    pe.wait_ge(s_mem_scaled, MC)
                    for c in range(DC):
                        if c >= 4:
                            pe.wait_ge(s_memT_tmp, c - 3)
                        for t in range(MC):
                            mm = pe.transpose(ps[:, c % 4, t * P:(t + 1) * P],
                                              mem_rows[:, t, c * P:(c + 1) * P], ident[:])
                        mm.then_inc(s_memT_ps, 1)
                elif step[0] == "tot":
                    if step[1] == 4:
                        pe.wait_ge(s_memT_tmp, DC)
                    norm_tot(step[1])
                elif step[0] == "bc":
                    norm_bc(step[1])
                elif step[0] == "S":
                    _, half, h = step
                    w = half * MHEADS + h
                    pe.wait_ge(b_free, b_first[("tile", B0[f"q{half}"] + HD * (h + 1) - 1)] + 1)
                    if w >= 1:
                        pe.wait_ge(s_exp, HT * w)
                    for t in range(HT):
                        tt = slice(t * P, (t + 1) * P)
                        for e in range(HD):
                            c = HD * h + e
                            mm = three(ps[:, t // 2, (t % 2) * MEM:(t % 2 + 1) * MEM],
                                       mq_hi[:, c, tt], mq_lo[:, c, tt], mk_hi[:, c, :], mk_lo[:, c, :],
                                       e == 0, e == HD - 1)
                    mm.then_inc(s_S, 1)
                elif step[0] == "T":
                    _, half, h = step
                    w = half * MHEADS + h
                    pe.wait_ge(s_prob, w + 1)
                    if w >= 1:
                        pe.wait_ge(s_pT, w)
                    for m in range(MC):
                        for t in range(HT):
                            mm = pe.transpose(ps[:, 2 + m, t * P:(t + 1) * P],
                                              prob[:, w % 2, t, m * P:(m + 1) * P], ident[:])
                    mm.then_inc(s_pT_ps, 1)
                elif step[0] == "PV":
                    _, half, h = step
                    w = half * MHEADS + h
                    pe.wait_ge(s_pT, w + 1)
                    for e in range(HD):
                        pe.wait_ge(b_free, k - 3)
                        ch = slice((HD * h + e) * P, (HD * h + e + 1) * P)
                        for m in range(MC):
                            mm = three(ps[:, 4 + k % 4, :], mv_hi[:, m, ch], mv_lo[:, m, ch],
                                       pT_hi[:, m, :], pT_lo[:, m, :], m == 0, m == MC - 1)
                        mm.then_inc(b_out, 1)
                        k += 1
            norm_tot(7)
            ffn(f2, final=True)

        @block.scalar
        def _(act):
            def copy(to, src, scale=1.0):
                return act.activation(to, src, ACT.Copy, scale=scale)

            def square(q, c, nth=None):
                nth = DC * q + c if nth is None else nth
                if nth >= 2:
                    act.wait_ge(s_ssq, nth - 1)
                act.activation(sq[:, nth % 2], xT[:, c, tok(q % 2)], ACT.Square).then_inc(s_sq, 1)

            def norm_std(q):
                act.wait_ge(s_var, q + 1)
                act.activation(std[:, q, :], var[:, q, :], ACT.Sqrt).then_inc(s_std, 1)

            def xn_hi(q, c):
                act.wait_ge(s_xn_tmp, DC * q + c + 1)
                copy(act_hi[:, c, tok(q % 2)], xn_tmp[:, c % 2]).then_inc(s_xn_hi, 1)

            def first_weights(F_):
                act.wait_ge(F_.gate_in, 16)
                copy(gate_hi[:], gate_raw[:]).then_inc(F_.gate_hi, 1)
                act.wait_ge(F_.up_in, 16)
                copy(up_hi[:], up_raw[:]).then_inc(F_.up_hi, 1)

            def ffn(F_):
                def chunk(c, parity, s, first=False, downs=True):
                    for half in range(2):
                        act.wait_ge(F_.gate_done, 2 * c + half + 1)
                        if not first:
                            act.wait_ge(F_.prod, 2 * c - 1 + half)
                        act.activation(silu[:, half], ps[:, half, :], ACT.Silu).then_inc(F_.silu, 1)
                    act.wait_ge(F_.gate_in, 16 * (c + 2))
                    copy(gate_hi[:], gate_raw[:]).then_inc(F_.gate_hi, 1)
                    for half in range(2):
                        act.wait_ge(F_.prod, 2 * c + half + 1)
                        copy(h_hi[:, 2 * parity + s, tok(half)], h_sum[:, half]).then_inc(F_.h_hi, 1)
                        if half == 0 and downs:
                            act.wait_ge(F_.down_in, 16 * (c - 1))
                            copy(down_hi[:, s], down_raw[:]).then_inc(F_.down_hi, 1)
                    act.wait_ge(F_.up_done, 2 * c + 2)
                    act.wait_ge(F_.up_in, 16 * (c + 2))
                    copy(up_hi[:], up_raw[:]).then_inc(F_.up_hi, 1)

                chunk(0, 0, 0, first=True, downs=False)
                chunk(1, 0, 1, downs=False)
                with act.Fori(0, (GROUPS - 1) // 2) as it:
                    for parity in (1, 0):
                        g = 2 * it + (1 if parity else 2)
                        act.wait_ge(F_.out_free, BANKS + 2 * DC * (g - 1))
                        chunk(2 * g, parity, 0)
                        chunk(2 * g + 1, parity, 1)

            act.wait_ge(s_gains_ps, 1)
            copy(gains[:], ps[:, 0, 0:GP + NG]).then_inc(s_gains, 1)
            for k in range(2 * DC):
                act.wait_ge(s_xt, k + 1)
                square(k // DC, k % DC)
                if k == DC - 1:
                    first_weights(f1)
            for q in range(2):
                norm_std(q)
                for c in range(DC):
                    xn_hi(q, c)
            ffn(f1)
            for step in tail_steps(2):
                if step[0] == "add":
                    k = step[1]
                    act.wait_ge(f1.out_free, BANKS + LAST + k + 1)
                    square(2 + k // DC, k % DC)
                elif step[0] == "tot":
                    norm_std(step[1])
                elif step[0] == "xn":
                    xn_hi(step[1], step[2])

            def a_weight(n):
                act.wait_ge(a_in[n % 2], 16 * (n // 2 + 1))
                if n >= 2:
                    act.wait_ge(a_out, a_through[n - 2])
                copy(wa_hi[:, n % 2], wa_raw[:, n % 2]).then_inc(a_hi, 1)

            def pool_hi_part(k):
                g, half = divmod(k, 2)
                act.wait_ge(s_pooled, g + 1)
                if k >= 2:
                    act.wait_ge(a_out, A_PROJ + k - 1)
                copy(pool_hi[:, half], pooled[:, g, tok(half)]).then_inc(s_pl_hi, 1)

            a_weight(0)
            a_weight(1)
            for c in range(DC):
                xn_hi(3, c)
            act.wait_ge(s_wp_in, 16)
            copy(wp_hi[:], wp_raw[:]).then_inc(s_wp_hi, 1)
            ahead, spill = 2, 0
            for k, (n, kind, j, part) in enumerate(A_UNITS):
                bank = ps[:, 4 + k % 4, :]
                if k == A_PROJ:
                    pool_hi_part(0)
                    pool_hi_part(1)
                if kind != "u":
                    act.wait_ge(a_out, k + 1)
                if kind == "pool":
                    copy(act_hi[:, DC // 2 + j, tok(part)], bank,
                         scale=gains[:, GP + j:GP + j + 1]).then_inc(a_ehi, 1)
                    if k - A_PROJ + 2 < 2 * NG:
                        pool_hi_part(k - A_PROJ + 2)
                elif kind == "v":
                    copy(v_hi[:, part, j * 2 * P:(j + 1) * 2 * P], bank[:, 0:2 * P]).then_inc(a_ehi, 1)
                elif kind in ("q", "k"):
                    if spill >= 2:
                        act.wait_ge(s_spill[part], 32 * (spill // 2))
                    copy(stage_hi[:, part], bank).then_inc(a_ehi, 1)
                    spill += 1
                while ahead < len(A_TILES) and a_through[ahead - 2] <= k + 1:
                    a_weight(ahead)
                    ahead += 1

            def b_weight(n):
                act.wait_ge(b_in[n % 2], 16 * (n // 2 + 1))
                if n >= 2:
                    act.wait_ge(b_out, b_through[n - 2])
                copy(wb_hi[:, n % 2], wb_raw[:, n % 2]).then_inc(b_hi, 1)

            for s in range(M + VALUE_LAG):
                if s < M:
                    n = (tile_at(s)[1] + 1) * P
                    act.wait_ge(s_z, s + 1)
                    z = ps[:, slice(*z_bank[s]), :].rearrange("p b n -> p (b n)")[:, 0:n]
                    if s >= 3:
                        act.wait_ge(s_a, s - 2)
                        if weighed(s - 3):
                            act.wait_ge(s_a_far, weighed(s - 3))
                    act.activation(rest[:, s % 3, 0:n], z, ACT.Sigmoid, scale=-SB_SCALE).then_inc(s_sig, 1)
                    if s >= 4:
                        act.wait_ge(s_aT_ps, turns_before[s - 3])
                    act.activation(beta[:, s % 4, 0:n], z, ACT.Sigmoid, scale=SB_SCALE).then_inc(s_sig, 1)
                m = s - TURN_LAG
                if 0 <= m < M:
                    for nth, bank, first, end in turns(m):
                        act.wait_ge(s_aT_ps, nth + 1)
                        if m % 2 == 0 and first == 0 and m >= 4:
                            act.wait_ge(s_o, m // 2 - 1)
                        copy(aT_part(aT_hi, m, first, end),
                             ps[:, bank, 0:(end - first) * P].rearrange("p (j t) -> p j t", t=P)
                             ).then_inc(s_aT_hi, 1)
                if s == M + 2:
                    b_weight(0)
                    b_weight(1)
                if s >= VALUE_LAG and (s - VALUE_LAG) % 2 == 0:
                    w = (s - VALUE_LAG) // 2
                    h, b = pair_at(w)
                    rows = slice(64 * (h % 2), 64 * (h % 2 + 1))
                    act.wait_ge(s_o, w + 1)
                    copy(act_hi[rows, h // 2, b * 2 * P:(b + 1) * 2 * P],
                         ps[rows, 7, (w % 2) * 2 * P:(w % 2 + 1) * 2 * P]).then_inc(s_o_hi, 1)

            ahead = 2
            for step in B_STEPS:
                k = b_first[step]
                if step[0] == "tile":
                    n = step[1]
                    kind, j, _ = B_TILES[n]
                    if kind == "mk":
                        act.wait_ge(b_out, k + 1)
                        copy(mk_hi[:, j, :], ps[:, 4 + k % 4, 0:MEM]).then_inc(b_ehi, 1)
                    elif kind == "mv" and j % 2:
                        for t in range(MC):
                            act.wait_ge(b_out, k + t + 1)
                            copy(mv_hi[:, t, (j - 1) * P:(j + 1) * P],
                                 ps[:, 4 + (k + t) % 4, 0:2 * P]).then_inc(b_ehi, 1)
                    elif kind in ("q0", "q1"):
                        act.wait_ge(b_out, k + 1)
                        copy(mq_hi[:, j, :], ps[:, 4 + k % 4, :]).then_inc(b_ehi, 1)
                    while ahead < len(B_TILES) and b_through[ahead - 2] <= b_through[n] and not (
                            kind == "mv" and j % 2 == 0):
                        b_weight(ahead)
                        ahead += 1
                    if kind in ADDS:
                        for i, half in enumerate(add_halves(kind)):
                            act.wait_ge(b_free, k + i + 1)
                            q = (4 if kind == "out" else 6) + half
                            square(q, j, nth=DC * 4 + 2 * j + half if kind == "out" else None)
                elif step[0] == "mem_rms":
                    act.wait_ge(s_mem_in, 16 * MC)
                    for c in range(MC):
                        if c:
                            act.wait_ge(s_mem_sq, c)
                        act.activation(mem_sq[:], mem_rows[:, c, :], ACT.Square,
                                       accum_out=mvar[:, 0, c:c + 1]).then_inc(s_mem_sq, 1)
                    act.wait_ge(s_mem_chain, 1)
                    act.activation(mvar[:, 2, :], mvar[:, 1, :], ACT.Sqrt).then_inc(s_mem_sq, 1)
                elif step[0] == "memT":
                    for c in range(DC):
                        act.wait_ge(s_memT_tmp, c + 1)
                        copy(memT_hi[:, c, :], mem_tmp[:, c % 2]).then_inc(s_memT_hi, 1)
                elif step[0] == "tot":
                    norm_std(step[1])
                elif step[0] == "xn":
                    xn_hi(step[1], step[2])
                elif step[0] == "S":
                    w = step[1] * MHEADS + step[2]
                    act.wait_ge(s_nmx, w + 1)
                    for t in range(HT):
                        act.activation(prob[:, w % 2, t, :], ps[:, t // 2, (t % 2) * MEM:(t % 2 + 1) * MEM],
                                       ACT.Exp, scale=MEM_SCALE, bias=mstat[:, w % 2, 1, t:t + 1],
                                       accum_out=mstat[:, w % 2, 2, t:t + 1]).then_inc(s_exp, 1)
                elif step[0] == "T":
                    _, half, h = step
                    w = half * MHEADS + h
                    act.wait_ge(s_pT_ps, w + 1)
                    if w >= 1:
                        act.wait_ge(b_out, b_first[pv_step(w - 1)] + HD)
                    copy(pT_hi[:].rearrange("p m t -> p (m t)"),
                         ps[:, 2:4, :].rearrange("p m t -> p (m t)")).then_inc(s_pT_hi, 1)
                elif step[0] == "PV":
                    _, half, h = step
                    for e in range(HD):
                        act.wait_ge(b_out, k + e + 1)
                        copy(act_hi[:, HD * h + e, tok(half)], ps[:, 4 + (k + e) % 4, :]).then_inc(b_ehi, 1)
            first_weights(f2)
            for c in range(DC):
                if c == 0:
                    norm_std(7)
                xn_hi(7, c)
            ffn(f2)
            for t in range(TC):
                act.wait_ge(s_yT, t + 1)
                if t:
                    act.wait_ge(s_ysq, t)
                act.activation(y_sq[:], ps[:, 2 * (t % 2):2 * (t % 2) + 2, :].rearrange("p b n -> p (b n)"),
                               ACT.Square, accum_out=fstat[:, 0, t:t + 1]).then_inc(s_ysq, 1)
                act.wait_ge(s_fchain, 6 * t + 1)
                act.activation(fstat[:, 2, t:t + 1], fstat[:, 1, t:t + 1], ACT.Sqrt).then_inc(s_fstd, 1)

        @block.vector
        def _(dve):
            def lo(to, value, hi):
                return dve.tensor_tensor(to, value, plain(hi), ALU.subtract)

            def newton(ms, root, cols_, chain, base):
                r, t, t2, y = cols_
                dve.reciprocal(r, root).then_inc(chain, 1)
                dve.wait_ge(chain, base + 1)
                dve.tensor_tensor(t, r, r, ALU.mult).then_inc(chain, 1)
                dve.wait_ge(chain, base + 2)
                dve.tensor_tensor(t2, t, ms, ALU.mult).then_inc(chain, 1)
                dve.wait_ge(chain, base + 3)
                dve.tensor_scalar(t, t2, -0.5, 1.5, ALU.mult, ALU.add).then_inc(chain, 1)
                dve.wait_ge(chain, base + 4)
                dve.tensor_tensor(y, r, t, ALU.mult).then_inc(chain, 1)
                dve.wait_ge(chain, base + 5)

            def norm_var(q):
                dve.wait_ge(s_tot, q + 1)
                dve.tensor_scalar(var[:, q, :], ps[:, q % 2, 0:2 * HT:2], 1.0 / D, EPS,
                                  ALU.mult, ALU.add).then_inc(s_var, 1)

            def norm_diag(q):
                dve.wait_ge(s_std, q + 1)
                newton(var[:, q, :], std[:, q, :], [rstd[:, q, i, :] for i in range(4)], s_chain, 5 * q)
                if q:
                    dve.wait_ge(s_bc, q)
                for j in range(HT):
                    ins = dve.tensor_scalar(diag[:, j * P:(j + 1) * P], ident[:], rstd[:, q, 3, j:j + 1], None,
                                            ALU.mult)
                ins.then_inc(s_diag, 1)

            def xn_lo(q, c):
                dve.wait_ge(s_xn_hi, DC * q + c + 1)
                lo(act_lo[:, c, tok(q % 2)], xn_tmp[:, c % 2], act_hi[:, c, tok(q % 2)]).then_inc(s_xn, 1)

            def xn(q, c):
                gain = {0: G1, 2: GM, 4: GQ, 6: G2}[q - q % 2]
                if c == 0:
                    dve.wait_ge(s_bc, q + 1)
                if DC * q + c >= 2:
                    dve.wait_ge(s_xn, DC * q + c - 1)
                dve.scalar_tensor_tensor(out=xn_tmp[:, c % 2], in0=xT[:, c, tok(q % 2)],
                                         scalar=gains[:, gain + c:gain + c + 1], in1=ps[:, 2 + q % 2, :],
                                         op0=ALU.mult, op1=ALU.mult).then_inc(s_xn_tmp, 1)
                if c:
                    xn_lo(q, c - 1)
                if c == DC - 1:
                    xn_lo(q, c)

            def first_weights(F_):
                dve.wait_ge(F_.gate_hi, 1)
                lo(gate_lo[:], gate_raw[:], gate_hi[:]).then_inc(F_.gate_lo, 1)
                dve.wait_ge(F_.up_hi, 1)
                lo(up_lo[:], up_raw[:], up_hi[:]).then_inc(F_.up_lo, 1)

            def add(F_, before, k):
                half, d = divmod(k, DC)
                dve.wait_ge(F_.out_done, before + k + 1)
                dve.scalar_tensor_tensor(out=xT[:, d, tok(half)], in0=ps[:, 4 + k % 4, :], scalar=0.5,
                                         in1=xT[:, d, tok(half)], op0=ALU.mult,
                                         op1=ALU.add).then_inc(F_.out_free, 1)

            def ffn(F_):
                def chunk(c, parity, s, first=False, downs=True):
                    dve.wait_ge(F_.gate_hi, c + 2)
                    lo(gate_lo[:], gate_raw[:], gate_hi[:]).then_inc(F_.gate_lo, 1)
                    for half in range(2):
                        dve.wait_ge(F_.up_done, 2 * c + half + 1)
                        dve.wait_ge(F_.silu, 2 * c + half + 1)
                        if not first:
                            dve.wait_ge(F_.h_lo, 2 * c - 1 + half)
                        dve.tensor_tensor(h_sum[:, half], silu[:, half], ps[:, 2 + half, :],
                                          ALU.mult).then_inc(F_.prod, 1)
                        dve.wait_ge(F_.h_hi, 2 * c + half + 1)
                        lo(h_lo[:, 2 * parity + s, tok(half)], h_sum[:, half],
                           h_hi[:, 2 * parity + s, tok(half)]).then_inc(F_.h_lo, 1)
                        if half == 0 and downs:
                            dve.wait_ge(F_.down_hi, c - 1)
                            lo(down_lo[:, s], down_raw[:], down_hi[:, s]).then_inc(F_.down_lo, 1)
                    dve.wait_ge(F_.up_hi, c + 2)
                    lo(up_lo[:], up_raw[:], up_hi[:]).then_inc(F_.up_lo, 1)

                dve.sem_inc(F_.out_free, BANKS)
                chunk(0, 0, 0, first=True, downs=False)
                chunk(1, 0, 1, downs=False)
                with dve.Fori(0, (GROUPS - 1) // 2) as it:
                    for parity in (1, 0):
                        g = 2 * it + (1 if parity else 2)
                        chunk(2 * g, parity, 0)
                        chunk(2 * g + 1, parity, 1)
                        dve.wait_ge(F_.out_free, BANKS + 2 * DC * (g - 1))
                        for k in range(2 * DC):
                            add(F_, 2 * DC * (g - 1), k)

            def final_rows(t):
                dve.wait_ge(s_ysq, t + 1)
                dve.tensor_scalar(fstat[:, 1, t:t + 1], fstat[:, 0, t:t + 1], 1.0 / D, EPS, ALU.mult,
                                  ALU.add).then_inc(s_fchain, 1)
                dve.wait_ge(s_fstd, t + 1)
                newton(fstat[:, 1, t:t + 1], fstat[:, 2, t:t + 1], [fstat[:, i, t:t + 1] for i in (3, 4, 5, 6)],
                       s_fchain, 6 * t + 1)
                if t == 0:
                    dve.wait_ge(s_fin_in, 16)
                if t >= 2:
                    dve.wait_ge(s_out[t % 2], 16 * (t // 2))
                dve.scalar_tensor_tensor(out=y_row[:, t % 2, :],
                                         in0=ps[:, 2 * (t % 2):2 * (t % 2) + 2, :].rearrange("p b n -> p (b n)"),
                                         scalar=fstat[:, 6, t:t + 1], in1=gain_all[:], op0=ALU.mult,
                                         op1=ALU.mult).then_inc(s_y, 1)

            for k in range(2 * DC):
                dve.wait_ge(s_xt_ps, k + 1)
                dve.tensor_copy(xT[:, k % DC, tok(k // DC)], ps[:, 4 + k % 4, :]).then_inc(s_xt, 1)
                if k == DC - 1:
                    first_weights(f1)
            dve.wait_ge(s_gains, 1)
            for q in range(2):
                norm_var(q)
                norm_diag(q)
                if q == 0:
                    for c in range(DC):
                        xn(q, c)
            for c in range(DC):
                xn(1, c)
            ffn(f1)
            dve.wait_ge(f1.out_free, BANKS + LAST)
            for step in tail_steps(2):
                if step[0] == "add":
                    add(f1, LAST, step[1])
                elif step[0] == "tot":
                    norm_var(step[1])
                    norm_diag(step[1])
                elif step[0] == "xn":
                    xn(step[1], step[2])

            def a_weight(n):
                dve.wait_ge(a_hi, n + 1)
                lo(wa_lo[:, n % 2], wa_raw[:, n % 2], wa_hi[:, n % 2]).then_inc(a_lo, 1)

            def pool_lo_part(k):
                g, half = divmod(k, 2)
                dve.wait_ge(s_pl_hi, k + 1)
                lo(pool_lo[:, half], pooled[:, g, tok(half)], pool_hi[:, half]).then_inc(s_pl, 1)

            a_weight(0)
            a_weight(1)
            for c in range(DC):
                xn(3, c)
            dve.wait_ge(s_wp_hi, 1)
            lo(wp_lo[:], wp_raw[:], wp_hi[:]).then_inc(s_wp, 1)
            dve.wait_ge(s_counts, PAD)
            dve.wait_ge(s_pads, 3)
            ahead, spill, links = 2, 0, 0
            for k, (n, kind, j, part) in enumerate(A_UNITS):
                bank = ps[:, 4 + k % 4, :]
                if k == A_PROJ:
                    pool_lo_part(0)
                    pool_lo_part(1)
                if kind == "u":
                    dve.wait_ge(a_out, k + 1)
                    if j:
                        dve.wait_ge(s_pooled, j)
                    dve.tensor_copy(u[:, PAD + part * HALF:PAD + (part + 1) * HALF], bank).then_inc(a_free, 1)
                else:
                    dve.wait_ge(a_ehi, k - A_U + 1)
                if kind == "pool":
                    to = act_lo[:, DC // 2 + j, tok(part)]
                    dve.scalar_tensor_tensor(out=to, in0=bank, scalar=gains[:, GP + j:GP + j + 1],
                                             in1=plain(act_hi[:, DC // 2 + j, tok(part)]), op0=ALU.mult,
                                             op1=ALU.subtract).then_inc(a_free, 1)
                    if k - A_PROJ + 2 < 2 * NG:
                        pool_lo_part(k - A_PROJ + 2)
                elif kind == "v":
                    c256 = slice(j * 2 * P, (j + 1) * 2 * P)
                    lo(v_lo[:, part, c256], bank[:, 0:2 * P], v_hi[:, part, c256]).then_inc(a_free, 1)
                elif kind in ("q", "k"):
                    if spill >= 2:
                        dve.wait_ge(s_spill[part], 32 * (spill // 2))
                    lo(stage_lo[:, part], bank, stage_hi[:, part]).then_inc(a_free, 1)
                    spill += 1
                while ahead < len(A_TILES) and a_through[ahead - 2] <= k + 1:
                    a_weight(ahead)
                    ahead += 1
                if kind == "u" and part == 1:
                    w = POOL_WINDOWS[j]
                    sums = (s0, s1)[j % 2]
                    dve.wait_ge(s_wsum, j + 1)
                    dve.wait_ge(a_free, k + 1)
                    dve.scalar_tensor_tensor(out=pooled[:, j, w:], in0=sums[:, PAD + w:], scalar=1.0 / w,
                                             in1=u[:, PAD + w:], op0=ALU.mult, op1=ALU.subtract)
                    dve.tensor_tensor(head_mean[:, 0:w], sums[:, PAD:PAD + w], recip_count[:, 0:w],
                                      ALU.mult).then_inc(s_dchain, 1)
                    dve.wait_ge(s_dchain, j + 1)
                    dve.tensor_tensor(pooled[:, j, 0:w], head_mean[:, 0:w], u[:, PAD:PAD + w],
                                      ALU.subtract).then_inc(s_pooled, 1)

            def b_weight(n):
                dve.wait_ge(b_hi, n + 1)
                lo(wb_lo[:, n % 2], wb_raw[:, n % 2], wb_hi[:, n % 2]).then_inc(b_lo, 1)

            def stick(m):
                n = (tile_at(m)[1] + 1) * P
                r = rest[:, m % 3, 0:n]
                dve.wait_ge(s_mask, 2 * (m + 1))
                dve.tensor_tensor_scan(r[:, ::-1], r[:, ::-1], r[:, ::-1], 1.0, ALU.mult,
                                       ALU.bypass).then_inc(s_scan, 1)
                if n > HALF:
                    dve.wait_ge(s_scan, m + 1)
                    dve.tensor_tensor(beta[:, m % 4, HALF:n - 1], beta[:, m % 4, HALF:n - 1],
                                      rest[:, m % 3, HALF + 1:n], ALU.mult).then_inc(s_a_far, 1)

            for s in range(M + VALUE_LAG):
                if 0 <= s - STICK_LAG < M:
                    stick(s - STICK_LAG)
                m = s - TURN_LAG
                if 0 <= m < M:
                    for nth, bank, first, end in turns(m):
                        dve.wait_ge(s_aT_hi, nth + 1)
                        lo(aT_part(aT_lo, m, first, end),
                           ps[:, bank, 0:(end - first) * P].rearrange("p (j t) -> p j t", t=P),
                           aT_part(aT_hi, m, first, end)).then_inc(s_aT, 1)
                if s == M + 2:
                    b_weight(0)
                    b_weight(1)
                if s >= VALUE_LAG and (s - VALUE_LAG) % 2 == 0:
                    w = (s - VALUE_LAG) // 2
                    h, b = pair_at(w)
                    at = (slice(64 * (h % 2), 64 * (h % 2 + 1)), h // 2, slice(b * 2 * P, (b + 1) * 2 * P))
                    dve.wait_ge(s_o_hi, w + 1)
                    lo(act_lo[at], ps[at[0], 7, (w % 2) * 2 * P:(w % 2 + 1) * 2 * P],
                       act_hi[at]).then_inc(s_o_free, 1)

            ahead = 2
            for step in B_STEPS:
                k = b_first[step]
                if step[0] == "tile":
                    n = step[1]
                    kind, j, _ = B_TILES[n]
                    if kind in ADDS:
                        for i, half in enumerate(add_halves(kind)):
                            dve.wait_ge(b_out, k + i + 1)
                            dve.tensor_tensor(xT[:, j, tok(half)], ps[:, 4 + (k + i) % 4, :], xT[:, j, tok(half)],
                                              ALU.add).then_inc(b_free, 1)
                    elif kind == "mk":
                        dve.wait_ge(b_ehi, b_hi_of[k] + 1)
                        lo(mk_lo[:, j, :], ps[:, 4 + k % 4, 0:MEM], mk_hi[:, j, :]).then_inc(b_free, 1)
                    elif kind == "mv" and j % 2:
                        for t in range(MC):
                            c256 = slice((j - 1) * P, (j + 1) * P)
                            dve.wait_ge(b_ehi, b_hi_of[k + t] + 1)
                            lo(mv_lo[:, t, c256], ps[:, 4 + (k + t) % 4, 0:2 * P],
                               mv_hi[:, t, c256]).then_inc(b_free, 1)
                    elif kind in ("q0", "q1"):
                        dve.wait_ge(b_ehi, b_hi_of[k] + 1)
                        lo(mq_lo[:, j, :], ps[:, 4 + k % 4, :], mq_hi[:, j, :]).then_inc(b_free, 1)
                    while ahead < len(B_TILES) and b_through[ahead - 2] <= b_through[n] and not (
                            kind == "mv" and j % 2 == 0):
                        b_weight(ahead)
                        ahead += 1
                elif step[0] == "mem_rms":
                    dve.wait_ge(s_mem_sq, MC)
                    dve.tensor_scalar(mvar[:, 1, :], mvar[:, 0, :], 1.0 / D, EPS, ALU.mult,
                                      ALU.add).then_inc(s_mem_chain, 1)
                    dve.wait_ge(s_mem_sq, MC + 1)
                    newton(mvar[:, 1, :], mvar[:, 2, :], [mvar[:, i, :] for i in (3, 4, 5, 6)], s_mem_chain, 1)
                    for c in range(MC):
                        dve.tensor_scalar(mem_rows[:, c, :], mem_rows[:, c, :], mvar[:, 6, c:c + 1], None,
                                          ALU.mult).then_inc(s_mem_scaled, 1)
                elif step[0] == "memT":
                    for c in range(DC + 1):
                        if c < DC:
                            dve.wait_ge(s_memT_ps, c + 1)
                            if c >= 2:
                                dve.wait_ge(s_memT, c - 1)
                            dve.tensor_scalar(mem_tmp[:, c % 2], ps[:, c % 4, 0:MEM],
                                              gains[:, GKV + c:GKV + c + 1], None,
                                              ALU.mult).then_inc(s_memT_tmp, 1)
                        if c:
                            dve.wait_ge(s_memT_hi, c)
                            lo(memT_lo[:, c - 1, :], mem_tmp[:, (c - 1) % 2],
                               memT_hi[:, c - 1, :]).then_inc(s_memT, 1)
                elif step[0] == "tot":
                    norm_var(step[1])
                    norm_diag(step[1])
                elif step[0] == "xn":
                    xn(step[1], step[2])
                elif step[0] == "S":
                    w = step[1] * MHEADS + step[2]
                    st = mstat[:, w % 2]
                    dve.wait_ge(s_S, w + 1)
                    dve.tensor_reduce(st[:, 0, :], ps[:, 0:2, :].rearrange("p b (t m) -> p (b t) m", m=MEM),
                                      AX_X, ALU.max).then_inc(s_mx, 1)
                    dve.wait_ge(s_mx, w + 1)
                    dve.tensor_scalar(st[:, 1, :], st[:, 0, :], -MEM_SCALE, None, ALU.mult).then_inc(s_nmx, 1)
                    dve.wait_ge(s_exp, HT * (w + 1))
                    dve.reciprocal(st[:, 3, :], st[:, 2, :]).then_inc(s_rinv, 1)
                    dve.wait_ge(s_rinv, w + 1)
                    for t in range(HT):
                        ins = dve.tensor_scalar(prob[:, w % 2, t, :], prob[:, w % 2, t, :], st[:, 3, t:t + 1], None,
                                                ALU.mult)
                    ins.then_inc(s_prob, 1)
                elif step[0] == "T":
                    _, half, h = step
                    w = half * MHEADS + h
                    dve.wait_ge(s_pT_hi, w + 1)
                    lo(pT_lo[:].rearrange("p m t -> p (m t)"), ps[:, 2:4, :].rearrange("p m t -> p (m t)"),
                       pT_hi[:].rearrange("p m t -> p (m t)")).then_inc(s_pT, 1)
                elif step[0] == "PV":
                    _, half, h = step
                    for e in range(HD):
                        dve.wait_ge(b_ehi, b_hi_of[k + e] + 1)
                        lo(act_lo[:, HD * h + e, tok(half)], ps[:, 4 + (k + e) % 4, :],
                           act_hi[:, HD * h + e, tok(half)]).then_inc(b_free, 1)
            first_weights(f2)
            norm_var(7)
            norm_diag(7)
            for c in range(DC):
                xn(7, c)
            ffn(f2)
            dve.wait_ge(f2.out_free, BANKS + LAST)
            for k in range(2 * DC):
                add(f2, LAST, k)
                if k >= DC + 1 and k % 2:
                    final_rows((k - DC) // 2)
            for t in range(HT, TC):
                final_rows(t)


_INS = ["x", "mem", "ffn1_norm", "ffn1_w_gate", "ffn1_w_up", "ffn1_w_down", "mix_norm", "w_in", "w_pool",
        "pool_scale", "w_out", "mem_q_norm", "mem_kv_norm", "mem_w_q", "mem_w_kv", "mem_w_o",
        "ffn2_norm", "ffn2_w_gate", "ffn2_w_up", "ffn2_w_down", "final_norm"]


def kernel(**inputs):
    import numpy as np
    from concourse import bacc
    from concourse.bass_utils import run_bass_kernel_spmd

    nc = bacc.Bacc("TRN2", target_bir_lowering=False, num_devices=1, dynamic_dma_scratch_size=1024)
    arrays, args = {}, []
    for name in _INS:
        a = np.ascontiguousarray(inputs[name])
        arrays[f"in_{name}"] = a
        args.append(nc.dram_tensor(f"in_{name}", a.shape, mybir.dt.from_np(a.dtype), kind="ExternalInput").ap())
    shape = arrays["in_x"].shape
    args.append(nc.dram_tensor("out_y", shape, F32, kind="ExternalOutput").ap())
    layer_program(nc, *args)
    result = run_bass_kernel_spmd(nc, [arrays], core_ids=[0])
    return result.results[0]["out_y"]
```

```python
from contextlib import ExitStack

import concourse.bass as bass
from concourse import mybir

ALU = mybir.AluOpType
ACT = mybir.ActivationFunctionType
F32 = mybir.dt.float32
F32R = mybir.dt.float32r
AX_X = mybir.AxisListType.X

P = 128
HALF = 512
EPS = 1e-6
POOL_WINDOWS = (2, 4, 8, 16)
PAD = max(POOL_WINDOWS)


def layer_program(nc, x, mem, ffn1_norm, ffn1_w_gate, ffn1_w_up, ffn1_w_down, mix_norm, w_in, w_pool,
                  pool_scale, w_out, mem_q_norm, mem_kv_norm, mem_w_q, mem_w_kv, mem_w_o,
                  ffn2_norm, ffn2_w_gate, ffn2_w_up, ffn2_w_down, final_norm, out):
    _, SEQ, D = x.shape
    MEM = mem.shape[1]
    F = ffn1_w_gate.shape[2]
    DC = D // P
    TC = SEQ // P
    HT = HALF // P
    FC = F // P
    GROUPS = FC // 2
    MC = MEM // P
    SBW = D // 2
    HEADS = SBW // 64
    SB_SCALE = 64 ** -0.5
    MHEADS = 4
    HD = D // MHEADS // P
    MEM_SCALE = (D // MHEADS) ** -0.5
    NG = len(POOL_WINDOWS)
    PAIR_ORDER = (0, 3, 1, 2)
    AT_BLOCKS = 12
    AT_FIRST = {0: 8, 3: 0, 1: 8, 2: 0}
    assert D == 1024 and SEQ == 2 * HALF and GROUPS % 2 == 1 and MC == 2

    ctx = ExitStack()
    with ctx:
        def sb(name, shape, dt=F32, into=ctx):
            return into.enter_context(nc.sbuf_tensor(name, shape, dt))

        def sem(name):
            return ctx.enter_context(nc.semaphore(name))

        def shared(name, kib, *sets):
            made = {}
            for tensors in sets:
                with ExitStack() as scope:
                    for n, shape, dt in tensors:
                        made[n] = sb(n, shape, dt, scope)
            sb(name, [P, kib * 256], F32)
            return made

        xT = sb("xT", [P, DC, SEQ])
        act_hi = sb("act_hi", [P, DC, SEQ], F32R)
        act_lo = sb("act_lo", [P, DC, SEQ], F32R)
        ident = sb("ident", [P, P])
        ones = sb("ones", [P, P])
        gain_rows = sb("gain_rows", [5 * DC + NG, P])
        gains = sb("gains", [P, 5 * DC + NG])
        recip_count = sb("recip_count", [P, PAD])
        sq = sb("sq", [P, 2, HALF])
        ssq = sb("ssq", [P, SEQ])
        xn_tmp = sb("xn_tmp", [P, 2, HALF])
        diag = sb("diag", [P, HALF])
        var = sb("var", [P, 8, HT])
        x_sq = sb("x_sq", [P, TC])
        std = sb("std", [P, 8, HT])
        rstd = sb("rstd", [P, 8, 4, HT])
        G1, GM, GQ, GKV, G2, GP = (DC * i for i in range(6))

        ffn_set = ExitStack()
        ffn_bufs = {}
        for n, shape, dt in (
            ("silu", [P, 2, HALF], F32), ("h_sum", [P, 2, HALF], F32),
            ("gain_all", [P, D], F32), ("y_row", [P, 2, D], F32), ("y_sq", [P, D], F32),
            ("gate_hi", [P, DC, P], F32R), ("gate_lo", [P, DC, P], F32R),
            ("up_hi", [P, DC, P], F32R), ("up_lo", [P, DC, P], F32R),
            ("gate_raw", [P, DC, P], F32), ("up_raw", [P, DC, P], F32), ("down_raw", [P, D], F32),
            ("down_hi", [P, 2, D], F32R), ("down_lo", [P, 2, D], F32R),
        ):
            ffn_bufs[n] = sb(n, shape, dt, ffn_set)
        with ExitStack() as scope:
            x_rows = sb("x_rows", [P, TC, D], F32, scope)
        h_hi = sb("h_hi", [P, 4, SEQ], F32R, ffn_set)
        h_lo = sb("h_lo", [P, 4, SEQ], F32R, ffn_set)
        ffn_set.close()
        silu, h_sum, gain_all, y_row, y_sq = (ffn_bufs[n] for n in ("silu", "h_sum", "gain_all", "y_row", "y_sq"))
        gate_hi, gate_lo, up_hi, up_lo = (ffn_bufs[n] for n in ("gate_hi", "gate_lo", "up_hi", "up_lo"))
        gate_raw, up_raw, down_raw = (ffn_bufs[n] for n in ("gate_raw", "up_raw", "down_raw"))
        down_hi, down_lo = ffn_bufs["down_hi"], ffn_bufs["down_lo"]

        r1 = shared("region1", 24,
                    [("wa_hi", [P, 2, DC, P], F32R), ("wa_lo", [P, 2, DC, P], F32R),
                     ("wa_raw", [P, 2, DC, P], F32)],
                    [("q_stack", [P, 2, SEQ], F32R), ("k_hi2", [P, 2, SEQ], F32R),
                     ("k_lo2", [P, 2, SEQ], F32R)],
                    [("wb_hi", [P, 2, DC, P], F32R), ("wb_lo", [P, 2, DC, P], F32R),
                     ("wb_raw", [P, 2, DC, P], F32)])
        r2 = shared("region2", 32,
                    [("v_hi", [P, TC, SBW], F32R), ("v_lo", [P, TC, SBW], F32R)],
                    [("memT_hi", [P, DC, MEM], F32R), ("memT_lo", [P, DC, MEM], F32R),
                     ("mem_rows", [P, MC, D], F32), ("mem_tmp", [P, 2, MEM], F32),
                     ("mem_sq", [P, D], F32)],
                    [("mq_hi", [P, DC, HALF], F32R), ("mq_lo", [P, DC, HALF], F32R)])
        r3 = shared("region3", 16,
                    [("pooled", [P, NG, SEQ], F32)],
                    [("beta", [P, 4, SEQ], F32)],
                    [("mk_hi", [P, DC, MEM], F32R), ("mk_lo", [P, DC, MEM], F32R)])
        r4 = shared("region4", 36,
                    [("u", [P, PAD + SEQ], F32), ("s0", [P, PAD + SEQ], F32), ("s1", [P, PAD + SEQ], F32),
                     ("pool_hi", [P, 2, HALF], F32R), ("pool_lo", [P, 2, HALF], F32R),
                     ("wp_raw", [P, NG, P], F32), ("wp_hi", [P, NG, P], F32R), ("wp_lo", [P, NG, P], F32R),
                     ("stage_hi", [P, 2, HALF], F32R), ("stage_lo", [P, 2, HALF], F32R),
                     ("head_mean", [P, PAD], F32)],
                    [("rest", [P, 3, SEQ], F32),
                     ("aT_hi", [P, AT_BLOCKS, 2 * P], F32R), ("aT_lo", [P, AT_BLOCKS, 2 * P], F32R)],
                    [("mv_hi", [P, MC, D], F32R), ("mv_lo", [P, MC, D], F32R),
                     ("prob", [P, 2, HT, MEM], F32),
                     ("pT_hi", [P, MC, HALF], F32R), ("pT_lo", [P, MC, HALF], F32R)])
        wa_hi, wa_lo, wa_raw = r1["wa_hi"], r1["wa_lo"], r1["wa_raw"]
        wb_hi, wb_lo, wb_raw = r1["wb_hi"], r1["wb_lo"], r1["wb_raw"]
        q_stack, k_hi2, k_lo2 = r1["q_stack"], r1["k_hi2"], r1["k_lo2"]
        v_hi, v_lo = r2["v_hi"], r2["v_lo"]
        memT_hi, memT_lo, mem_rows, mem_tmp, mem_sq = (
            r2["memT_hi"], r2["memT_lo"], r2["mem_rows"], r2["mem_tmp"], r2["mem_sq"])
        mq_hi, mq_lo = r2["mq_hi"], r2["mq_lo"]
        pooled, mk_hi, mk_lo = r3["pooled"], r3["mk_hi"], r3["mk_lo"]
        u, s0, s1, head_mean = r4["u"], r4["s0"], r4["s1"], r4["head_mean"]
        pool_hi, pool_lo = r4["pool_hi"], r4["pool_lo"]
        wp_raw, wp_hi, wp_lo = r4["wp_raw"], r4["wp_hi"], r4["wp_lo"]
        stage_hi, stage_lo = r4["stage_hi"], r4["stage_lo"]
        beta, rest, aT_hi, aT_lo = r3["beta"], r4["rest"], r4["aT_hi"], r4["aT_lo"]
        mv_hi, mv_lo, prob, pT_hi, pT_lo = r4["mv_hi"], r4["mv_lo"], r4["prob"], r4["pT_hi"], r4["pT_lo"]
        mstat = sb("mstat", [P, 2, 4, HT])
        mvar = sb("mvar", [P, 8, MC])
        fstat = sb("fstat", [P, 8, TC])

        q_spill_hi = nc.dram_tensor("q_spill_hi", [SBW, SEQ], F32).ap()
        q_spill_lo = nc.dram_tensor("q_spill_lo", [SBW, SEQ], F32).ap()
        k_spill_hi = nc.dram_tensor("k_spill_hi", [SBW, SEQ], F32).ap()
        k_spill_lo = nc.dram_tensor("k_spill_lo", [SBW, SEQ], F32).ap()

        ps = ctx.enter_context(nc.psum_tensor("ps", [P, 8, HALF], F32))

        s_const, s_counts = sem("s_const"), sem("s_counts")
        s_rows_in = sem("s_rows_in")
        s_gains_ps, s_gains = sem("s_gains_ps"), sem("s_gains")
        s_x_in = [sem(f"s_x_in{t}") for t in range(TC)]
        s_row_sq = sem("s_row_sq")
        s_xt_ps = sem("s_xt_ps")
        s_xt, s_xt_a = sem("s_xt"), sem("s_xt_a")
        s_sq, s_ssq, s_tot, s_var, s_std = sem("s_sq"), sem("s_ssq"), sem("s_tot"), sem("s_var"), sem("s_std")
        s_chain, s_diag, s_bc = sem("s_chain"), sem("s_diag"), sem("s_bc")
        s_xn_tmp, s_xn_hi, s_xn = sem("s_xn_tmp"), sem("s_xn_hi"), sem("s_xn")

        class Ffn:
            def __init__(self, tag, gate, up, down, norm):
                self.gate, self.up, self.down = gate[0], up[0], down[0]
                self.norm = norm
                (self.gate_in, self.up_in, self.down_in,
                 self.gate_hi, self.gate_lo, self.up_hi, self.up_lo,
                 self.down_hi, self.down_lo,
                 self.gate_done, self.up_done,
                 self.silu, self.prod, self.h_hi, self.h_lo,
                 self.out_done, self.out_free) = (
                    sem(f"{tag}_{n}") for n in (
                        "gate_in", "up_in", "down_in", "gate_hi", "gate_lo", "up_hi", "up_lo", "down_hi",
                        "down_lo", "gate_done", "up_done", "silu", "prod", "h_hi", "h_lo",
                        "out_done", "out_free"))

        f1 = Ffn("f1", ffn1_w_gate, ffn1_w_up, ffn1_w_down, 0)
        f2 = Ffn("f2", ffn2_w_gate, ffn2_w_up, ffn2_w_down, 6)
        BANKS = 4
        LAST = 2 * DC * (GROUPS - 1)

        a_in = [sem("a_in0"), sem("a_in1")]
        a_hi, a_lo = sem("a_hi"), sem("a_lo")
        a_half = sem("a_half")
        a_out, a_ehi, a_free = sem("a_out"), sem("a_ehi"), sem("a_free")
        s_wsum, s_pooled, s_pads, s_pchain, s_dchain = (
            sem("s_wsum"), sem("s_pooled"), sem("s_pads"), sem("s_pchain"), sem("s_dchain"))
        s_wp_in, s_wp_hi, s_wp = sem("s_wp_in"), sem("s_wp_hi"), sem("s_wp")
        s_pl_hi, s_pl = sem("s_pl_hi"), sem("s_pl")
        s_spill = [sem("s_spill0"), sem("s_spill1")]
        s_stack = [sem("s_stack0"), sem("s_stack1")]
        s_z, s_sig, s_mask, s_scan = sem("s_z"), sem("s_sig"), sem("s_mask"), sem("s_scan")
        s_a, s_a_far = sem("s_a"), sem("s_a_far")
        s_aT_ps, s_aT_hi, s_aT = sem("s_aT_ps"), sem("s_aT_hi"), sem("s_aT")
        s_o, s_o_hi, s_o_free = sem("s_o"), sem("s_o_hi"), sem("s_o_free")

        b_in = [sem("b_in0"), sem("b_in1")]
        b_hi, b_lo = sem("b_hi"), sem("b_lo")
        b_half = sem("b_half")
        b_out, b_ehi, b_free = sem("b_out"), sem("b_ehi"), sem("b_free")
        s_mem_in, s_mem_sq, s_mem_chain, s_mem_scaled = (
            sem("s_mem_in"), sem("s_mem_sq"), sem("s_mem_chain"), sem("s_mem_scaled"))
        s_memT_ps, s_memT_tmp, s_memT_hi, s_memT = (
            sem("s_memT_ps"), sem("s_memT_tmp"), sem("s_memT_hi"), sem("s_memT"))
        s_S, s_mx, s_nmx, s_exp, s_rinv, s_prob = (
            sem("s_S"), sem("s_mx"), sem("s_nmx"), sem("s_exp"), sem("s_rinv"), sem("s_prob"))
        s_pT_ps, s_pT_hi, s_pT = sem("s_pT_ps"), sem("s_pT_hi"), sem("s_pT")
        s_fin_in, s_yT, s_ysq, s_fvar, s_fchain, s_fstd, s_y = (
            sem("s_fin_in"), sem("s_yT"), sem("s_ysq"), sem("s_fvar"), sem("s_fchain"), sem("s_fstd"), sem("s_y"))
        s_out = [sem("s_out0"), sem("s_out1")]

        Y_BANK = (0, 2, 0, 2, 4, 6, 0, 2)
        BC_BANK = (6, 7, 2, 3, 2, 3, 2, 6)
        X_BY_ACT, X_BANKS = (6, 7, 4, 5), (1, 3, 4, 5)

        def tok(half):
            return slice(half * HALF, (half + 1) * HALF)

        def cols(w, n):
            return w[:, n * P:(n + 1) * P].rearrange("(c p) m -> p c m", p=P)

        def wide_cols(w, n):
            rows = slice((n % 2) * D // 2, (n % 2 + 1) * D // 2)
            return w[rows, (n // 2) * 2 * P:(n // 2 + 1) * 2 * P].rearrange("(e p) m -> p e m", p=P)

        def wide(buf, slot):
            return buf[:, slot].rearrange("p c m -> p (c m)").rearrange("p (e m) -> p e m", m=2 * P)

        def plain(ap):
            return ap.bitcast(F32)

        wi = w_in[0]
        A_TILES = [("q", 0), ("k", 0), ("u", 0), ("q", 1), ("u", 1), ("k", 1), ("u", 2), ("q", 2), ("u", 3),
                   ("k", 2), ("v", 0), ("v", 1), ("v", 2), ("v", 3), ("q", 3), ("k", 3)]
        a_column = {"q": 0, "k": SBW, "v": 2 * SBW, "u": 3 * SBW}
        a_units, a_work, a_empty, a_done, u_done = [], [("pair", 0, 0), ("pair", 1, 2)], [], [], []
        for half in range(2):
            for n in range(2):
                a_units.append((*A_TILES[n], half))
                a_empty.append(("unit", len(a_units) - 1))
                if half:
                    a_empty.append(("split", n + 2))
                    a_done.append(len(a_units))
        late = []
        for n, (kind, j) in enumerate(A_TILES):
            if n < 2:
                continue
            k = len(a_units)
            if kind == "v":
                a_work.append(("wide", n, k))
                parts = range(TC) if j % 2 else ()
            else:
                a_work += [("unit", n, half, k + half) for half in range(2)]
                parts = range(2)
            a_units += [(kind, j, part) for part in parts]
            a_empty += [("unit", k + part) for part in parts]
            a_done.append(len(a_units) if parts else None)
            if n + 2 < len(A_TILES):
                a_empty.append(("split", n + 2))
            a_empty += late
            late = [("mean", j)] if kind == "u" else []
            if kind == "u":
                u_done.append(len(a_units))
        A_PROJ = len(a_units)
        a_units += [("pool", g, half) for g in range(NG) for half in range(2)]
        pool_first = range(A_PROJ, A_PROJ + 6)
        pool_among = [range(0), range(A_PROJ + 6, A_PROJ + 7), range(A_PROJ + 7, A_PROJ + 8)]
        a_empty += [("unit", k) for k in pool_first]
        a_slot, slot = [], 0
        for kind, _, _ in a_units:
            a_slot.append(slot)
            slot = 1 - slot if kind in ("q", "k") else slot
        a_bank, a_after, a_hi_of, ring, holds = [], [], [], 0, {}
        for k, (kind, j, part) in enumerate(a_units):
            if kind == "v":
                bank = (part + 4) % TC
            else:
                bank, ring = 4 + ring, (ring + 1) % 4
            a_after.append(holds.get(bank, 0))
            holds[bank] = k + 1
            if bank < 4:
                z_banks_free = k + 1
            a_bank.append(bank)
            a_hi_of.append(sum(u[0] != "u" for u in a_units[:k]))

        mem_k, mem_v = mem_w_kv[0][:, 0:D], mem_w_kv[0][:, D:2 * D]
        b_source = {"out0": w_out[0], "out1": w_out[0], "mk": mem_k, "q0": mem_w_q[0], "q1": mem_w_q[0],
                    "o0": mem_w_o[0], "o1": mem_w_o[0]}

        def tiles(kind, lo, hi):
            return [("tile", kind, j) for j in range(lo, hi)]

        def xn_steps(q, lo, hi):
            return [("xn", q, c) for c in range(lo, hi)]

        B_STEPS = tiles("out0", 0, 1) + [("mem_rms",)] + tiles("out0", 1, 3) + [("memT",)] + tiles("out0", 3, DC)
        for j in range(0, DC, 2):
            B_STEPS += tiles("mk", j, j + 1) + [("tot", 4)] * (j == 0) + tiles("mk", j + 1, j + 2)
            B_STEPS += tiles("out1", j, j + 1) + [("bc", 4)] * (j == 0)
            B_STEPS += tiles("mv", j, j + 2) + xn_steps(4, j, j + 1)
            B_STEPS += tiles("out1", j + 1, j + 2) + xn_steps(4, j + 1, j + 2)
        B_STEPS += tiles("q0", 0, 1) + [("tot", 5)] + tiles("q0", 1, 2) + [("bc", 5)]
        for j in range(2, DC):
            B_STEPS += xn_steps(5, *((2 * j - 4, 2 * j - 2) if j < 4 else (j, j + 1))) + tiles("q0", j, j + 1)
        for h in range(MHEADS):
            B_STEPS += [("S", 0, h)] + tiles("q1", HD * h, HD * h + 1) + [("T", 0, h)]
            B_STEPS += tiles("q1", HD * h + 1, HD * (h + 1)) + [("PV", 0, h)]
        for h in range(MHEADS):
            B_STEPS += [("S", 1, h)] + tiles("o0", HD * h, HD * h + 1) + [("T", 1, h)]
            B_STEPS += tiles("o0", HD * h + 1, HD * (h + 1)) + [("PV", 1, h)]
        B_STEPS += tiles("o1", 0, 1) + [("tot", 6)] + tiles("o1", 1, 2) + [("bc", 6)]
        for j in range(2, DC - 2):
            B_STEPS += xn_steps(6, 2 * j - 4, 2 * j - 2) + tiles("o1", j, j + 1)
        B_STEPS += [("ffn",)] + tiles("o1", DC - 2, DC)
        B_TILES = [step for step in B_STEPS if step[0] == "tile"]
        b_tile = {step: n for n, step in enumerate(B_TILES)}
        ADDS = ("out0", "out1", "o0", "o1")
        b_first, b_hi_of, n_units, n_hi = {}, {}, 0, 0
        for step in B_STEPS:
            b_first[step] = n_units
            made = {"PV": HD, "tile": 1}.get(step[0], 0)
            if step[:2] == ("tile", "mv"):
                made = MC * (step[2] % 2)
            for k in range(n_units, n_units + made):
                b_hi_of[k] = n_hi
                n_hi += step[0] == "PV" or step[1] not in ADDS
            n_units += made

        def pv_step(w):
            return ("PV", w // MHEADS, w % MHEADS)

        def tail_steps(q):
            steps = [("hi", 0), ("hi", 1)]
            for k in range(2 * DC):
                steps.append(("add", k))
                if k < 2:
                    steps.append(("lo", k))
                if k == DC + 2:
                    steps += [("tot", q), ("var", q), ("diag", q)]
                if k == DC + 5:
                    steps.append(("bc", q))
                if k >= DC + 6:
                    steps.append(("xn", q, k - DC - 6))
            steps += [("xn", q, c) for c in range(DC - 6, 5)]
            return steps + [("var", q + 1), ("xn", q, 5), ("diag", q + 1), ("xn", q, 6), ("xn", q, 7)]

        Y_STEPS = [(step, t) for t in range(HT) for step in ("mean", "std", "rows")]
        Y_STEPS += [("mean", HT)]
        for t in range(HT, TC):
            Y_STEPS += [("mean", t + 1)] * (t + 1 < TC) + [("std", t), ("rows", t)]

        M = HEADS * TC
        W = M // 2
        turns_before = [0]
        for m in range(M):
            i = 2 * PAIR_ORDER[m % TC // 2] + m % 2
            turns_before.append(turns_before[-1] + i // 4 + 1)

        def tile_at(m):
            return m // TC, 2 * PAIR_ORDER[m % TC // 2] + m % 2

        def pair_at(w):
            return w // (TC // 2), PAIR_ORDER[w % (TC // 2)]

        z_bank, z_free_after = [], []
        holds = {}
        for m in range(M):
            i, first = tile_at(m)[1], (z_bank[-1][1] % 4 if m else 0)
            z_bank.append((first, first + i // 4 + 1))
            z_free_after.append(max([holds.get(b, -1) + 1 for b in range(*z_bank[m])]))
            holds.update((b, m) for b in range(*z_bank[m]))
        assert all(end <= 4 for _, end in z_bank)

        def weighed(m):
            return sum(tile_at(k)[1] >= 4 for k in range(m + 1))

        def turns(m):
            i = tile_at(m)[1]
            return [(turns_before[m] + n, 4 + (turns_before[m] + n) % 3, 4 * n, min(4 * n + 4, i + 1))
                    for n in range(i // 4 + 1)]

        def aT_part(buf, m, begin, end):
            first = AT_FIRST[tile_at(m)[1] // 2]
            return buf[:, first + begin:first + end, (m % 2) * P:(m % 2 + 1) * P]

        STICK_LAG, TURN_LAG, VALUE_LAG = 1, 3, 6

        block = ctx.enter_context(nc.Block())

        @block.sync
        def _(sp):
            def x_load(t):
                sp.dma_start(x_rows[:, t, :], x[0, t * P:(t + 1) * P, :]).then_inc(s_x_in[t], 16)

            for t in range(HT):
                x_load(t)

            def ffn_loads(F_, between=None):
                def gate_up(c, first=False):
                    if not first:
                        sp.wait_ge(F_.gate_lo, c)
                    sp.dma_start(gate_raw[:], F_.gate[:, bass.ds(c * P, P)]
                                 .rearrange("(c p) m -> p c m", p=P)).then_inc(F_.gate_in, 16)
                    if not first:
                        sp.wait_ge(F_.up_lo, c)
                    sp.dma_start(up_raw[:], F_.up[:, bass.ds(c * P, P)]
                                 .rearrange("(c p) m -> p c m", p=P)).then_inc(F_.up_in, 16)

                def down(c, first=False):
                    if not first:
                        sp.wait_ge(F_.down_lo, c)
                    sp.dma_start(down_raw[:], F_.down[bass.ds(c * P, P), :]).then_inc(F_.down_in, 16)

                gate_up(0, first=True)
                if between:
                    between()
                gate_up(1)
                gate_up(2)
                down(0, first=True)
                with sp.Fori(0, FC - 3) as it:
                    gate_up(it + 3)
                    down(it + 1)
                sp.wait_ge(F_.gate_lo, FC)
                sp.dma_start(gate_raw[:].rearrange("p c m -> p (c m)"),
                             F_.down[(FC - 2) * P:(FC - 1) * P, :]).then_inc(F_.gate_in, 16)
                sp.wait_ge(F_.up_lo, FC)
                sp.dma_start(up_raw[:].rearrange("p c m -> p (c m)"),
                             F_.down[(FC - 1) * P:, :]).then_inc(F_.up_in, 16)

            ffn_loads(f1, between=lambda: [x_load(t) for t in range(HT, TC)])

            def stack_load(h):
                if h < 2:
                    sp.wait_ge(a_out, a_done[h - 2])
                else:
                    sp.wait_ge(s_z, TC * (h - 1))
                if h in (0, HEADS - 2):
                    for slot in range(2):
                        sp.wait_ge(s_spill[slot], 32 * (2 * SBW // P - (2 if h == 0 else 0)))
                rows = slice(64 * h, 64 * (h + 1))
                for to, lower, upper in ((q_stack, q_spill_hi, q_spill_lo), (k_hi2, k_spill_hi, k_spill_hi),
                                         (k_lo2, k_spill_lo, k_spill_lo)):
                    sp.dma_start(plain(to[0:64, h % 2]), lower[rows, :]).then_inc(s_stack[h % 2], 16)
                    sp.dma_start(plain(to[64:P, h % 2]), upper[rows, :]).then_inc(s_stack[h % 2], 16)

            sp.wait_ge(f1.h_lo, 2 * FC)
            for n in range(len(A_TILES) + 4):
                if n == 4:
                    sp.wait_ge(f1.out_done, 2 * DC * GROUPS)
                    sp.dma_start(wp_raw[:], w_pool[0].rearrange("g p m -> p g m")).then_inc(s_wp_in, 16)
                for k, (kind, j, half) in enumerate(a_units[:A_PROJ]):
                    if n >= 4 and n != 5 and kind in ("q", "k") and (
                            k < 4 if n == 4 else A_TILES[n - 4] == (kind, j)):
                        to_hi, to_lo = (q_spill_hi, q_spill_lo) if kind == "q" else (k_spill_hi, k_spill_lo)
                        sp.wait_ge(a_free, k + 1)
                        slot = a_slot[k]
                        sp.dma_start(to_hi[j * P:(j + 1) * P, tok(half)],
                                     plain(stage_hi[:, slot])).then_inc(s_spill[slot], 16)
                        sp.dma_start(to_lo[j * P:(j + 1) * P, tok(half)],
                                     plain(stage_lo[:, slot])).then_inc(s_spill[slot], 16)
                if n < len(A_TILES):
                    kind, j = A_TILES[n]
                    if n >= 2:
                        sp.wait_ge(a_lo, n - 1)
                    if kind == "v":
                        src, to = wide_cols(wi[:, a_column["v"]:], j), wide(wa_raw, n % 2)
                    else:
                        src, to = cols(wi, a_column[kind] // P + j), wa_raw[:, n % 2]
                    sp.dma_start(to, src).then_inc(a_in[n % 2], 16)
                if n == len(A_TILES) + 2:
                    stack_load(0)
            for h in range(1, HEADS):
                stack_load(h)

            sp.wait_ge(s_z, M)
            for n, (_, kind, j) in enumerate(B_TILES):
                if n >= 2:
                    sp.wait_ge(b_lo, n - 1)
                if kind == "mv":
                    sp.dma_start(wide(wb_raw, n % 2), wide_cols(mem_v, j)).then_inc(b_in[n % 2], 16)
                else:
                    sp.dma_start(wb_raw[:, n % 2], cols(b_source[kind], j)).then_inc(b_in[n % 2], 16)
                if n == 1:
                    sp.wait_ge(s_o, W)
                    for c in range(MC):
                        sp.dma_start(mem_rows[:, c, :], mem[0, c * P:(c + 1) * P, :]).then_inc(s_mem_in, 16)

            sp.wait_ge(s_S, 2 * MHEADS)
            sp.wait_ge(b_free, b_first[pv_step(2 * MHEADS - 1)] + HD)
            ffn_loads(f2)
            sp.wait_ge(b_out, n_units)
            sp.dma_start(gain_all[:], final_norm.rearrange("(a d) -> a d", a=1)
                         .broadcast_to([P, D])).then_inc(s_fin_in, 16)
            for t in range(TC):
                sp.wait_ge(s_y, t + 1)
                sp.dma_start(out[0, t * P:(t + 1) * P, :], y_row[:, t % 2, :]).then_inc(s_out[t % 2], 16)
            for slot in range(2):
                sp.wait_ge(s_out[slot], 16 * TC // 2)

        @block.gpsimd
        def _(pool):
            pool.memset(ident[:], 0.0).then_inc(s_const, 1)
            pool.wait_ge(s_const, 1)
            pool.affine_select(out=ident[:], in_=ident[:], compare_op=ALU.not_equal, fill=1.0, base=0,
                               pattern=[[-1, P]], channel_multiplier=1).then_inc(s_const, 1)
            pool.memset(ones[:], 1.0).then_inc(s_const, 1)
            for t in range(PAD):
                pool.memset(recip_count[:, t:t + 1], 1.0 / (t + 1)).then_inc(s_counts, 1)

            pool.wait_ge(f1.up_hi, 1)
            pool.tensor_tensor(up_lo[:], up_raw[:], plain(up_hi[:]), ALU.subtract).then_inc(f1.up_lo, 1)

            def sum_squares(q, c):
                nth = DC * (q - 2) + c
                total = ssq[:, tok(q % 2)]
                if c == 0:
                    return
                pool.wait_ge(s_sq, nth + 1)
                if c == 1:
                    if q >= 4:
                        pool.wait_ge(s_tot, q - 3)
                    pool.tensor_tensor(total, sq[:, 0], sq[:, 1], ALU.add).then_inc(s_ssq, 2)
                else:
                    pool.wait_ge(s_ssq, nth)
                    pool.tensor_tensor(total, total, sq[:, nth % 2], ALU.add).then_inc(s_ssq, 1)

            for q in range(2, 4):
                for c in range(DC):
                    sum_squares(q, c)

            pool.wait_ge(f1.out_done, 2 * DC * GROUPS)
            for buf in (u, s0, s1):
                pool.memset(buf[:, 0:PAD], 0.0).then_inc(s_pads, 1)
            pool.wait_ge(s_pads, 3)
            links = 0
            for g, w in enumerate(POOL_WINDOWS):
                pool.wait_ge(a_free, u_done[g])
                if g:
                    pool.wait_ge(s_pooled, g)
                src, step, k = u, 1, 0
                while step < w:
                    dst = (s0, s1)[k % 2]
                    ins = pool.tensor_tensor(dst[:, PAD:], src[:, PAD:], src[:, PAD - step:PAD + SEQ - step],
                                             ALU.add)
                    step, src, k = 2 * step, dst, k + 1
                    if step < w:
                        links += 1
                        ins.then_inc(s_pchain, 1)
                        pool.wait_ge(s_pchain, links)
                    else:
                        ins.then_inc(s_wsum, 1)

            def mask(m):
                i = tile_at(m)[1]
                for nth, (buf, slot, fill) in enumerate(((rest, m % 3, 1.0), (beta, m % 4, 0.0))):
                    diagonal = buf[:, slot, i * P:(i + 1) * P]
                    pool.wait_ge(s_sig, 2 * m + nth + 1)
                    pool.affine_select(out=diagonal, in_=diagonal,
                                       compare_op=ALU.is_gt, fill=fill, base=0, pattern=[[-1, P]],
                                       channel_multiplier=1).then_inc(s_mask, 1)

            def weigh(m):
                n = min((tile_at(m)[1] + 1) * P, HALF + 1)
                pool.wait_ge(s_mask, 2 * (m + 1))
                pool.wait_ge(s_scan, m + 1)
                pool.tensor_tensor(beta[:, m % 4, 0:n - 1], beta[:, m % 4, 0:n - 1], rest[:, m % 3, 1:n],
                                   ALU.mult).then_inc(s_a, 1)

            for s in range(M + 1):
                if s < M:
                    mask(s)
                if s >= 1:
                    weigh(s - 1)

            for q in range(4, 8):
                for c in range(DC):
                    sum_squares(q, c)

        @block.tensor
        def _(pe):
            def three(to, w_hi, w_lo, m_hi, m_lo, first, last):
                pe.matmul(to, w_lo, m_hi, start=first, stop=False)
                pe.matmul(to, w_hi, m_lo, start=False, stop=False)
                return pe.matmul(to, w_hi, m_hi, start=False, stop=last)

            def norm_tot(q):
                pe.wait_ge(s_ssq, DC * (q - 1))
                half = q % 2
                for j in range(HT):
                    mm = pe.matmul(ps[:, half, 2 * j:2 * j + 2],
                                   ssq[:, half * HALF + j * P:half * HALF + (j + 1) * P],
                                   ones[:, 0:2], start=True, stop=True)
                mm.then_inc(s_tot, 1)

            def norm_bc(q):
                pe.wait_ge(s_diag, q + 1)
                pe.matmul(ps[:, BC_BANK[q], :], ones[:], diag[:], start=True, stop=True).then_inc(s_bc, 1)

            def pair(ways, ready, norm, together, between={}):
                def chunk(w, d):
                    to, hi, lo, done, half = ways[w]
                    mm = three(to, hi(d), lo(d), act_hi[:, d, tok(half)], act_lo[:, d, tok(half)],
                               d == 0, d == DC - 1)
                    if d == DC - 1:
                        mm.then_inc(done, 1)

                for d in range(together):
                    pe.wait_ge(s_xn, DC * norm + d + 1)
                    for w in range(2):
                        if d == 0:
                            pe.wait_ge(*ready[w])
                        chunk(w, d)
                    if d in between:
                        between[d]()
                for w in range(2):
                    for d in range(together, DC):
                        if w == 0:
                            pe.wait_ge(s_xn, DC * norm + d + 1)
                        chunk(w, d)

            pe.wait_ge(s_const, 3)

            def x_turn(t, c, bank, last):
                mm = pe.transpose(ps[:, bank, (t % HT) * P:(t % HT + 1) * P],
                                  x_rows[:, t, c * P:(c + 1) * P], ident[:])
                if last:
                    mm.then_inc(s_xt_ps, 1)

            for t in range(HT):
                pe.wait_ge(s_x_in[t], 16)
                for c in range(DC):
                    x_turn(t, c, c, t == HT - 1)
            pe.wait_ge(s_rows_in, 16 * 6)
            pe.wait_ge(s_xt, 1)
            rows = GP + NG
            pe.transpose(ps[:, 0, 0:rows], gain_rows[:], ident[0:rows, 0:rows]).then_inc(s_gains_ps, 1)
            pe.wait_ge(s_xt_a, X_BY_ACT.index(BC_BANK[0]) + 1)
            norm_bc(0)

            def x_turns(begin, end):
                for c in range(begin, end):
                    bank = X_BANKS[c % 4]
                    if c >= 4:
                        pe.wait_ge(s_xt_a, HT + c - 3)
                    elif bank in X_BY_ACT:
                        pe.wait_ge(s_xt_a, X_BY_ACT.index(bank) + 1)
                    else:
                        pe.wait_ge(s_xt, bank + 1)
                    for t in range(HT, TC):
                        if c == 0:
                            pe.wait_ge(s_x_in[t], 16)
                        x_turn(t, c, bank, t == TC - 1)

            def ffn(F_, final):
                def product(c, which, half):
                    whi, wlo, ready, done, busy = (
                        (gate_hi, gate_lo, F_.gate_lo, F_.gate_done, F_.silu),
                        (up_hi, up_lo, F_.up_lo, F_.up_done, F_.prod))[which]
                    pe.wait_ge(ready, c + 1)
                    pe.wait_ge(busy, 2 * c - 1 + half)
                    for d in range(DC):
                        mm = three(ps[:, 2 * which + half, :], whi[:, d, :], wlo[:, d, :],
                                   act_hi[:, d, tok(half)], act_lo[:, d, tok(half)], d == 0, d == DC - 1)
                    mm.then_inc(done, 1)

                def gate_up(c):
                    for which in range(2):
                        for half in range(2):
                            product(c, which, half)

                def down(g, parity):
                    pe.wait_ge(F_.down_lo, 2 * g + 2)
                    pe.wait_ge(F_.h_lo, 4 * g + 4)
                    for k in range(2 * DC):
                        half, d = divmod(k, DC)
                        pe.wait_ge(F_.out_free, 2 * DC * g + k + 1)
                        for s in range(2):
                            blk = slice(d * P, (d + 1) * P)
                            mm = three(ps[:, 4 + k % 4, :], down_hi[:, s, blk], down_lo[:, s, blk],
                                       h_hi[:, 2 * parity + s, tok(half)], h_lo[:, 2 * parity + s, tok(half)],
                                       s == 0, s == 1)
                        mm.then_inc(F_.out_done, 1)

                def first(half, together, between):
                    pair([(ps[:, half, :], lambda d: gate_hi[:, d, :], lambda d: gate_lo[:, d, :],
                           F_.gate_done, half),
                          (ps[:, 2 + half, :], lambda d: up_hi[:, d, :], lambda d: up_lo[:, d, :],
                           F_.up_done, half)],
                         [(F_.gate_lo, 1), (F_.up_lo, 1)], F_.norm + half, together, between)

                if F_.norm == 0:
                    pe.wait_ge(s_gains, 1)
                    pe.wait_ge(s_xt, 3)
                    first(0, DC, {5: lambda: x_turns(0, 4)})
                    pe.wait_ge(s_xt_a, X_BY_ACT.index(BC_BANK[1]) + 1)
                    norm_bc(1)
                    x_turns(4, DC)
                    pe.wait_ge(s_xt_a, HT + 6)
                else:
                    first(0, DC, {2: lambda: norm_tot(F_.norm + 1), 6: lambda: norm_bc(F_.norm + 1)})
                first(1, DC // 2, {})
                gate_up(1)
                with pe.Fori(0, (GROUPS - 1) // 2) as it:
                    for parity in (1, 0):
                        g = 2 * it + (1 if parity else 2)
                        gate_up(2 * g)
                        gate_up(2 * g + 1)
                        down(g - 1, 1 - parity)

                pe.wait_ge(F_.gate_lo, FC + 1)
                pe.wait_ge(F_.up_lo, FC + 1)
                pe.wait_ge(F_.h_lo, 2 * FC)

                def output(k):
                    half, d = divmod(k, DC)
                    pe.wait_ge(F_.out_free, LAST + k + 1)
                    for s, (whi, wlo) in enumerate(((gate_hi, gate_lo), (up_hi, up_lo))):
                        mm = three(ps[:, 4 + k % 4, :], whi[:, d, :], wlo[:, d, :],
                                   h_hi[:, s, tok(half)], h_lo[:, s, tok(half)], s == 0, s == 1)
                    mm.then_inc(F_.out_done, 1)

                if final:
                    for k in range(2 * DC):
                        output(k)
                        if k >= DC + 1 and k % 2:
                            y_turn((k - DC) // 2)
                    for t in range(HT, TC):
                        y_turn(t)
                else:
                    for step in tail_steps(2):
                        if step[0] == "add":
                            output(step[1])
                        elif step[0] == "tot":
                            norm_tot(step[1])
                        elif step[0] == "bc":
                            norm_bc(step[1])

            def y_turn(t):
                pe.wait_ge(f2.out_free, BANKS + LAST + DC * (t // HT + 1))
                if t in (2, 3, 6, 7):
                    pe.wait_ge(s_y, t - 1 if t < HT else t - 3)
                for c in range(DC):
                    mm = pe.transpose(ps[:, Y_BANK[t] + c // 4, (c % 4) * P:(c % 4 + 1) * P],
                                      xT[:, c, t * P:(t + 1) * P], ident[:])
                mm.then_inc(s_yT, 1)

            ffn(f1, final=False)

            def a_emptied(k):
                if a_after[k]:
                    pe.wait_ge(a_free, a_after[k])

            for step in a_work:
                if step[0] == "pair":
                    _, half, k = step
                    pair([(ps[:, a_bank[k + n], :], lambda d, n=n: wa_hi[:, n, d, :],
                           lambda d, n=n: wa_lo[:, n, d, :], a_out, half) for n in range(2)],
                         [(a_lo, 1), (a_lo, 2)], 2 + half, DC if half == 0 else DC // 2,
                         {1: lambda: norm_tot(3), 6: lambda: norm_bc(3)} if half == 0 else {})
                elif step[0] == "unit":
                    _, n, half, k = step
                    pe.wait_ge(a_lo, n + 1)
                    a_emptied(k)
                    for d in range(DC):
                        mm = three(ps[:, a_bank[k], :], wa_hi[:, n % 2, d, :], wa_lo[:, n % 2, d, :],
                                   act_hi[:, d, tok(half)], act_lo[:, d, tok(half)], d == 0, d == DC - 1)
                    mm.then_inc(a_out, 1)
                else:
                    _, n, k = step
                    second = A_TILES[n][1] % 2
                    pe.wait_ge(a_lo, n + 1)
                    for t in range(TC):
                        if not second:
                            a_emptied(k + t)
                        for e in range(DC // 2):
                            d = DC // 2 * second + e
                            tt = slice(t * P, (t + 1) * P)
                            mm = three(ps[:, a_bank[k + t], 0:2 * P], act_hi[:, d, tt], act_lo[:, d, tt],
                                       wide(wa_hi, n % 2)[:, e], wide(wa_lo, n % 2)[:, e], d == 0, d == DC - 1)
                        if second:
                            mm.then_inc(a_out, 1)
                    if not second:
                        mm.then_inc(a_half, 1)
            pe.wait_ge(s_wp, 1)
            def pool_map(k):
                _, g, half = a_units[k]
                a_emptied(k)
                pe.wait_ge(s_pl, k - A_PROJ + 1)
                three(ps[:, a_bank[k], :], wp_hi[:, g, :], wp_lo[:, g, :],
                      pool_hi[:, half], pool_lo[:, half], True, True).then_inc(a_out, 1)

            for k in pool_first:
                pool_map(k)

            def scores(m):
                h, i = tile_at(m)
                if m % TC == 0:
                    pe.wait_ge(s_stack[h % 2], 96 * (h // 2 + 1))
                if z_free_after[m]:
                    pe.wait_ge(s_sig, 2 * z_free_after[m])
                n = (i + 1) * P
                for lo in range(0, n, HALF):
                    keys = slice(lo, min(n, lo + HALF))
                    z = ps[:, z_bank[m][0] + lo // HALF, 0:keys.stop - lo]
                    pe.matmul(z, q_stack[:, h % 2, i * P:(i + 1) * P], k_lo2[:, h % 2, keys],
                              start=True, stop=False)
                    mm = pe.matmul(z, q_stack[:, h % 2, i * P:(i + 1) * P], k_hi2[:, h % 2, keys],
                                   start=False, stop=True)
                mm.then_inc(s_z, 1)

            def turn(m):
                pe.wait_ge(s_a, m + 1)
                if weighed(m):
                    pe.wait_ge(s_a_far, weighed(m))
                for nth, bank, first, end in turns(m):
                    if nth >= 3:
                        pe.wait_ge(s_aT, nth - 2)
                    for j in range(first, end):
                        mm = pe.transpose(ps[:, bank, (j - first) * P:(j - first + 1) * P],
                                          beta[:, m % 4, j * P:(j + 1) * P], ident[:])
                    mm.then_inc(s_aT_ps, 1)

            def values(w):
                h, b = pair_at(w)
                pe.wait_ge(s_aT, turns_before[2 * w + 2])
                if w:
                    pe.wait_ge(s_o_free, w)
                pair = slice((h // 2) * P, (h // 2 + 1) * P)
                o = ps[:, 7, (w % 2) * 2 * P:(w % 2 + 1) * 2 * P]
                for j in range(2 * b + 2):
                    lo = P if j == 2 * b + 1 else 0
                    block = AT_FIRST[b] + j
                    mm = three(o[:, lo:], v_hi[:, j, pair], v_lo[:, j, pair],
                               aT_hi[:, block, lo:], aT_lo[:, block, lo:], j == 0, j == 2 * b + 1)
                mm.then_inc(s_o, 1)

            pe.wait_ge(a_free, z_banks_free)
            for s in range(M + VALUE_LAG):
                if s < M:
                    scores(s)
                if s < TURN_LAG:
                    for k in pool_among[s]:
                        pool_map(k)
                if s == TURN_LAG:
                    pe.wait_ge(a_free, len(a_units))
                if 0 <= s - TURN_LAG < M:
                    turn(s - TURN_LAG)
                if s >= VALUE_LAG and (s - VALUE_LAG) % 2 == 0:
                    values((s - VALUE_LAG) // 2)

            pe.wait_ge(s_aT, turns_before[M])
            pe.wait_ge(s_o_free, W - 2)
            for step in B_STEPS:
                k = b_first[step]
                if step[0] == "tile":
                    _, kind, j = step
                    n = b_tile[step]
                    pe.wait_ge(b_lo, n + 1)
                    if kind == "mk" and j == 0:
                        pe.wait_ge(s_memT, DC)
                    if kind == "o0" and j == 0:
                        pe.wait_ge(b_free, b_first[pv_step(MHEADS - 1)] + HD)
                    if kind == "o1" and j == 0:
                        pe.wait_ge(b_free, b_first[pv_step(2 * MHEADS - 1)] + HD)
                    if kind == "mv":
                        for t in range(MC):
                            if j % 2 == 0:
                                pe.wait_ge(b_free, k + t - 3)
                            for e in range(DC // 2):
                                d = DC // 2 * (j % 2) + e
                                tt = slice(t * P, (t + 1) * P)
                                mm = three(ps[:, 4 + (k + t) % 4, 0:2 * P], memT_hi[:, d, tt], memT_lo[:, d, tt],
                                           wide(wb_hi, n % 2)[:, e], wide(wb_lo, n % 2)[:, e],
                                           d == 0, d == DC - 1)
                            if j % 2:
                                mm.then_inc(b_out, 1)
                        if j % 2 == 0:
                            mm.then_inc(b_half, 1)
                        continue
                    if k >= 4:
                        pe.wait_ge(b_free, k - 3)
                    bank = ps[:, 4 + k % 4, :]
                    order = [*range(DC // 2, DC), *range(DC // 2)] if kind == "out0" else range(DC)
                    for d in order:
                        ends = d == order[0], d == order[-1]
                        if n == 0 and d == DC // 2 - 1:
                            pe.wait_ge(s_o_free, W)
                        if kind == "mk":
                            mm = three(bank[:, 0:MEM], wb_hi[:, n % 2, d, :], wb_lo[:, n % 2, d, :],
                                       memT_hi[:, d, :], memT_lo[:, d, :], *ends)
                            continue
                        half = int(kind[-1])
                        if kind in ("q0", "q1") and j == 0:
                            pe.wait_ge(s_xn, DC * (4 + half) + d + 1)
                        mm = three(bank, wb_hi[:, n % 2, d, :], wb_lo[:, n % 2, d, :],
                                   act_hi[:, d, tok(half)], act_lo[:, d, tok(half)], *ends)
                    mm.then_inc(b_out, 1)
                elif step[0] == "memT":
                    pe.wait_ge(s_mem_scaled, MC)
                    for c in range(DC):
                        if c >= 4:
                            pe.wait_ge(s_memT_tmp, c - 3)
                        for t in range(MC):
                            mm = pe.transpose(ps[:, c % 4, t * P:(t + 1) * P],
                                              mem_rows[:, t, c * P:(c + 1) * P], ident[:])
                        mm.then_inc(s_memT_ps, 1)
                elif step[0] == "tot":
                    if step[1] == 4:
                        pe.wait_ge(s_memT_tmp, DC)
                    norm_tot(step[1])
                elif step[0] == "bc":
                    norm_bc(step[1])
                elif step[0] == "S":
                    _, half, h = step
                    w = half * MHEADS + h
                    pe.wait_ge(b_free, b_first[("tile", f"q{half}", HD * (h + 1) - 1)] + 1)
                    if w >= 1:
                        pe.wait_ge(s_exp, HT * w)
                    for t in range(HT):
                        tt = slice(t * P, (t + 1) * P)
                        for e in range(HD):
                            c = HD * h + e
                            mm = three(ps[:, t // 2, (t % 2) * MEM:(t % 2 + 1) * MEM],
                                       mq_hi[:, c, tt], mq_lo[:, c, tt], mk_hi[:, c, :], mk_lo[:, c, :],
                                       e == 0, e == HD - 1)
                    mm.then_inc(s_S, 1)
                elif step[0] == "T":
                    _, half, h = step
                    w = half * MHEADS + h
                    pe.wait_ge(s_prob, w + 1)
                    if w >= 1:
                        pe.wait_ge(s_pT, w)
                    for m in range(MC):
                        for t in range(HT):
                            mm = pe.transpose(ps[:, 2 + m, t * P:(t + 1) * P],
                                              prob[:, w % 2, t, m * P:(m + 1) * P], ident[:])
                    mm.then_inc(s_pT_ps, 1)
                elif step[0] == "PV":
                    _, half, h = step
                    w = half * MHEADS + h
                    pe.wait_ge(s_pT, w + 1)
                    for e in range(HD):
                        pe.wait_ge(b_free, k - 3)
                        ch = slice((HD * h + e) * P, (HD * h + e + 1) * P)
                        for m in range(MC):
                            mm = three(ps[:, 4 + k % 4, :], mv_hi[:, m, ch], mv_lo[:, m, ch],
                                       pT_hi[:, m, :], pT_lo[:, m, :], m == 0, m == MC - 1)
                        mm.then_inc(b_out, 1)
                        k += 1
            ffn(f2, final=True)

        @block.scalar
        def _(act):
            def copy(to, src, scale=1.0):
                return act.activation(to, src, ACT.Copy, scale=scale)

            def square(q, c):
                nth = DC * (q - 2) + c
                if nth >= 2:
                    act.wait_ge(s_ssq, nth - 1)
                act.activation(sq[:, nth % 2], xT[:, c, tok(q % 2)], ACT.Square).then_inc(s_sq, 1)

            def norm_std(q):
                act.wait_ge(s_var, q + 1)
                act.activation(std[:, q, :], var[:, q, :], ACT.Sqrt).then_inc(s_std, 1)

            def xn_hi(q, c):
                act.wait_ge(s_xn_tmp, DC * q + c + 1)
                copy(act_hi[:, c, tok(q % 2)], xn_tmp[:, c % 2]).then_inc(s_xn_hi, 1)

            def first_weights(F_):
                act.wait_ge(F_.gate_in, 16)
                copy(gate_hi[:], gate_raw[:]).then_inc(F_.gate_hi, 1)
                act.wait_ge(F_.up_in, 16)
                copy(up_hi[:], up_raw[:]).then_inc(F_.up_hi, 1)

            def ffn(F_):
                def chunk(c, parity, s, first=False, downs=True):
                    for half in range(2):
                        act.wait_ge(F_.gate_done, 2 * c + half + 1)
                        if not first:
                            act.wait_ge(F_.prod, 2 * c - 1 + half)
                        act.activation(silu[:, half], ps[:, half, :], ACT.Silu).then_inc(F_.silu, 1)
                    act.wait_ge(F_.gate_in, 16 * (c + 2))
                    copy(gate_hi[:], gate_raw[:]).then_inc(F_.gate_hi, 1)
                    for half in range(2):
                        act.wait_ge(F_.prod, 2 * c + half + 1)
                        copy(h_hi[:, 2 * parity + s, tok(half)], h_sum[:, half]).then_inc(F_.h_hi, 1)
                        if half == 0 and downs:
                            act.wait_ge(F_.down_in, 16 * (c - 1))
                            copy(down_hi[:, s], down_raw[:]).then_inc(F_.down_hi, 1)
                    act.wait_ge(F_.up_done, 2 * c + 2)
                    act.wait_ge(F_.up_in, 16 * (c + 2))
                    copy(up_hi[:], up_raw[:]).then_inc(F_.up_hi, 1)

                chunk(0, 0, 0, first=True, downs=False)
                chunk(1, 0, 1, downs=False)
                with act.Fori(0, (GROUPS - 1) // 2) as it:
                    for parity in (1, 0):
                        g = 2 * it + (1 if parity else 2)
                        act.wait_ge(F_.out_free, BANKS + 2 * DC * (g - 1))
                        chunk(2 * g, parity, 0)
                        chunk(2 * g + 1, parity, 1)

            for i, w in enumerate((ffn1_norm, mix_norm, mem_q_norm, mem_kv_norm, ffn2_norm)):
                act.dma_start(gain_rows[DC * i:DC * (i + 1), :],
                              w.rearrange("a (c p) -> (a c) p", p=P)).then_inc(s_rows_in, 16)
            act.dma_start(gain_rows[GP:GP + NG, :],
                          pool_scale.rearrange("a (c p) -> (a c) p", p=P)).then_inc(s_rows_in, 16)
            def row_square(t):
                act.wait_ge(s_x_in[t], 16)
                act.wait_ge(s_row_sq, t + 1)
                act.activation(sq[:].rearrange("p a n -> p (a n)"), x_rows[:, t, :], ACT.Square,
                               accum_out=x_sq[:, t:t + 1]).then_inc(s_row_sq, 1)

            act.wait_ge(s_const, 3)
            act.activation(x_sq[:, 0:1], ones[:, 0:1], ACT.Square).then_inc(s_row_sq, 1)
            for t in range(HT):
                row_square(t)
            norm_std(0)
            for c in X_BY_ACT:
                act.wait_ge(s_xt_ps, c + 1)
                copy(xT[:, c, tok(0)], ps[:, c, :]).then_inc(s_xt_a, 1)
            act.wait_ge(s_gains_ps, 1)
            copy(gains[:], ps[:, 0, 0:GP + NG]).then_inc(s_gains, 1)
            first_weights(f1)

            def x_copy(c):
                act.wait_ge(s_xt_ps, DC + c + 1)
                copy(xT[:, c, tok(1)], ps[:, X_BANKS[c % 4], :]).then_inc(s_xt_a, 1)

            for c in range(DC):
                xn_hi(0, c)
                if c in (1, 3, 5, 6):
                    row_square(HT + (1, 3, 5, 6).index(c))
            norm_std(1)
            for c in range(6):
                x_copy(c)
            for c in range(DC):
                xn_hi(1, c)
                if c < 2:
                    x_copy(6 + c)
            def a_weight(n):
                act.wait_ge(a_in[n % 2], 16 * (n // 2 + 1))
                if n >= 2:
                    if a_done[n - 2] is None:
                        act.wait_ge(a_half, A_TILES[n - 2][1] // 2 + 1)
                    else:
                        act.wait_ge(a_out, a_done[n - 2])
                copy(wa_hi[:, n % 2], wa_raw[:, n % 2]).then_inc(a_hi, 1)

            ffn(f1)
            for step in tail_steps(2):
                if step[0] == "add":
                    k = step[1]
                    act.wait_ge(f1.out_free, BANKS + LAST + k + 1)
                    square(2 + k // DC, k % DC)
                elif step[0] == "hi":
                    a_weight(step[1])
                elif step[0] == "var":
                    norm_std(step[1])
                elif step[0] == "xn":
                    xn_hi(step[1], step[2])

            def pool_hi_part(k):
                g, half = divmod(k, 2)
                act.wait_ge(s_pooled, g + 1)
                if k >= 2:
                    act.wait_ge(a_out, A_PROJ + k - 1)
                copy(pool_hi[:, half], pooled[:, g, tok(half)]).then_inc(s_pl_hi, 1)

            spills = [0, 0]

            def empty(step):
                if step == ("split", 4):
                    act.wait_ge(s_wp_in, 16)
                    copy(wp_hi[:], wp_raw[:]).then_inc(s_wp_hi, 1)
                if step[0] == "split":
                    a_weight(step[1])
                if step[0] != "unit":
                    return
                k = step[1]
                kind, j, part = a_units[k]
                bank = ps[:, a_bank[k], :]
                if k == A_PROJ - 2:
                    pool_hi_part(0)
                    pool_hi_part(1)
                if kind != "u":
                    act.wait_ge(a_out, k + 1)
                if kind == "pool":
                    copy(act_hi[:, DC // 2 + j, tok(part)], bank,
                         scale=gains[:, GP + j:GP + j + 1]).then_inc(a_ehi, 1)
                    if k - A_PROJ + 2 < 2 * NG:
                        pool_hi_part(k - A_PROJ + 2)
                elif kind == "v":
                    copy(v_hi[:, part, (j - 1) * P:(j + 1) * P], bank[:, 0:2 * P]).then_inc(a_ehi, 1)
                elif kind in ("q", "k"):
                    slot = a_slot[k]
                    if spills[slot]:
                        act.wait_ge(s_spill[slot], 32 * spills[slot])
                    copy(stage_hi[:, slot], bank).then_inc(a_ehi, 1)
                    spills[slot] += 1

            for c in range(DC):
                xn_hi(3, c)
                if c == 1:
                    for step in a_empty[:2]:
                        empty(step)
            for step in a_empty[2:]:
                empty(step)

            def b_weight(n):
                act.wait_ge(b_in[n % 2], 16 * (n // 2 + 1))
                if n >= 2:
                    before = B_TILES[n - 2]
                    if before[1] == "mv" and before[2] % 2 == 0:
                        act.wait_ge(b_half, before[2] // 2 + 1)
                    else:
                        act.wait_ge(b_out, b_first[before] + (MC if before[1] == "mv" else 1))
                copy(wb_hi[:, n % 2], wb_raw[:, n % 2]).then_inc(b_hi, 1)

            for s in range(M + VALUE_LAG):
                if s < M:
                    n = (tile_at(s)[1] + 1) * P
                    act.wait_ge(s_z, s + 1)
                    z = ps[:, slice(*z_bank[s]), :].rearrange("p b n -> p (b n)")[:, 0:n]
                    if s >= 3:
                        act.wait_ge(s_a, s - 2)
                        if weighed(s - 3):
                            act.wait_ge(s_a_far, weighed(s - 3))
                    act.activation(rest[:, s % 3, 0:n], z, ACT.Sigmoid, scale=-SB_SCALE).then_inc(s_sig, 1)
                    if s < NG:
                        act.wait_ge(s_pl, 2 * (s + 1))
                    if s >= 4:
                        act.wait_ge(s_aT_ps, turns_before[s - 3])
                    act.activation(beta[:, s % 4, 0:n], z, ACT.Sigmoid, scale=SB_SCALE).then_inc(s_sig, 1)
                if s < TURN_LAG:
                    for k in pool_among[s]:
                        empty(("unit", k))
                m = s - TURN_LAG
                if m == 0:
                    for slot in range(2):
                        act.wait_ge(s_spill[slot], 32 * (2 * SBW // P))
                if 0 <= m < M:
                    for nth, bank, first, end in turns(m):
                        act.wait_ge(s_aT_ps, nth + 1)
                        if m % 2 == 0 and first == 0 and m >= 4:
                            act.wait_ge(s_o, m // 2 - 1)
                        copy(aT_part(aT_hi, m, first, end),
                             ps[:, bank, 0:(end - first) * P].rearrange("p (j t) -> p j t", t=P)
                             ).then_inc(s_aT_hi, 1)
                if s >= VALUE_LAG and (s - VALUE_LAG) % 2 == 0:
                    w = (s - VALUE_LAG) // 2
                    h, b = pair_at(w)
                    rows = slice(64 * (h % 2), 64 * (h % 2 + 1))
                    act.wait_ge(s_o, w + 1)
                    copy(act_hi[rows, h // 2, b * 2 * P:(b + 1) * 2 * P],
                         ps[rows, 7, (w % 2) * 2 * P:(w % 2 + 1) * 2 * P]).then_inc(s_o_hi, 1)
                if s == M + 2:
                    b_weight(0)
                    b_weight(1)

            for step in B_STEPS:
                k = b_first[step]
                if step[0] == "tile":
                    _, kind, j = step
                    if kind == "mk":
                        act.wait_ge(b_out, k + 1)
                        copy(mk_hi[:, j, :], ps[:, 4 + k % 4, 0:MEM]).then_inc(b_ehi, 1)
                    elif kind == "mv" and j % 2:
                        for t in range(MC):
                            act.wait_ge(b_out, k + t + 1)
                            copy(mv_hi[:, t, (j - 1) * P:(j + 1) * P],
                                 ps[:, 4 + (k + t) % 4, 0:2 * P]).then_inc(b_ehi, 1)
                    elif kind in ("q0", "q1"):
                        act.wait_ge(b_out, k + 1)
                        copy(mq_hi[:, j, :], ps[:, 4 + k % 4, :]).then_inc(b_ehi, 1)
                    if b_tile[step] + 2 < len(B_TILES):
                        b_weight(b_tile[step] + 2)
                    if kind in ADDS:
                        act.wait_ge(b_free, k + 1)
                        square((4 if kind[:-1] == "out" else 6) + int(kind[-1]), j)
                elif step[0] == "mem_rms":
                    act.wait_ge(s_mem_in, 16 * MC)
                    for c in range(MC):
                        if c:
                            act.wait_ge(s_mem_sq, c)
                        act.activation(mem_sq[:], mem_rows[:, c, :], ACT.Square,
                                       accum_out=mvar[:, 0, c:c + 1]).then_inc(s_mem_sq, 1)
                    act.wait_ge(s_mem_chain, 1)
                    act.activation(mvar[:, 2, :], mvar[:, 1, :], ACT.Sqrt).then_inc(s_mem_sq, 1)
                elif step[0] == "memT":
                    for c in range(DC):
                        act.wait_ge(s_memT_tmp, c + 1)
                        copy(memT_hi[:, c, :], mem_tmp[:, c % 2]).then_inc(s_memT_hi, 1)
                elif step[0] == "ffn":
                    first_weights(f2)
                elif step[0] == "tot":
                    norm_std(step[1])
                elif step[0] == "xn":
                    xn_hi(step[1], step[2])
                elif step[0] == "S":
                    w = step[1] * MHEADS + step[2]
                    act.wait_ge(s_nmx, w + 1)
                    for t in range(HT):
                        act.activation(prob[:, w % 2, t, :], ps[:, t // 2, (t % 2) * MEM:(t % 2 + 1) * MEM],
                                       ACT.Exp, scale=MEM_SCALE, bias=mstat[:, w % 2, 1, t:t + 1],
                                       accum_out=mstat[:, w % 2, 2, t:t + 1]).then_inc(s_exp, 1)
                elif step[0] == "T":
                    _, half, h = step
                    w = half * MHEADS + h
                    act.wait_ge(s_pT_ps, w + 1)
                    if w >= 1:
                        act.wait_ge(b_out, b_first[pv_step(w - 1)] + HD)
                    copy(pT_hi[:].rearrange("p m t -> p (m t)"),
                         ps[:, 2:4, :].rearrange("p m t -> p (m t)")).then_inc(s_pT_hi, 1)
                elif step[0] == "PV":
                    _, half, h = step
                    for e in range(HD):
                        act.wait_ge(b_out, k + e + 1)
                        copy(act_hi[:, HD * h + e, tok(half)], ps[:, 4 + (k + e) % 4, :]).then_inc(b_ehi, 1)
            for c in range(DC):
                if c == 0:
                    norm_std(7)
                xn_hi(7, c)
            ffn(f2)
            def row_mean(t):
                act.wait_ge(s_yT, t + 1)
                if t:
                    act.wait_ge(s_ysq, t)
                act.activation(y_sq[:], ps[:, Y_BANK[t]:Y_BANK[t] + 2, :].rearrange("p b n -> p (b n)"),
                               ACT.Square, accum_out=fstat[:, 0, t:t + 1]).then_inc(s_ysq, 1)

            def row_std(t):
                act.wait_ge(s_fvar, t + 1)
                act.activation(fstat[:, 2, t:t + 1], fstat[:, 1, t:t + 1], ACT.Sqrt).then_inc(s_fstd, 1)

            for step, t in Y_STEPS:
                if step == "mean":
                    row_mean(t)
                elif step == "std":
                    row_std(t)

        @block.vector
        def _(dve):
            def lo(to, value, hi):
                return dve.tensor_tensor(to, value, plain(hi), ALU.subtract)

            def newton(ms, root, columns, chain, base):
                r, t, t2, y = columns
                dve.reciprocal(r, root).then_inc(chain, 1)
                dve.wait_ge(chain, base + 1)
                dve.tensor_tensor(t, r, r, ALU.mult).then_inc(chain, 1)
                dve.wait_ge(chain, base + 2)
                dve.tensor_tensor(t2, t, ms, ALU.mult).then_inc(chain, 1)
                dve.wait_ge(chain, base + 3)
                dve.tensor_scalar(t, t2, -0.5, 1.5, ALU.mult, ALU.add).then_inc(chain, 1)
                dve.wait_ge(chain, base + 4)
                dve.tensor_tensor(y, r, t, ALU.mult).then_inc(chain, 1)
                dve.wait_ge(chain, base + 5)

            def norm_var(q):
                if q < 2:
                    dve.wait_ge(s_row_sq, HT * (q + 1) + 1)
                    src = x_sq[:, HT * q:HT * (q + 1)]
                else:
                    dve.wait_ge(s_tot, q - 1)
                    src = ps[:, q % 2, 0:2 * HT:2]
                dve.tensor_scalar(var[:, q, :], src, 1.0 / D, EPS, ALU.mult, ALU.add).then_inc(s_var, 1)

            def norm_diag(q):
                dve.wait_ge(s_std, q + 1)
                newton(var[:, q, :], std[:, q, :], [rstd[:, q, i, :] for i in range(4)], s_chain, 5 * q)
                if q:
                    dve.wait_ge(s_bc, q)
                for j in range(HT):
                    ins = dve.tensor_scalar(diag[:, j * P:(j + 1) * P], ident[:], rstd[:, q, 3, j:j + 1], None,
                                            ALU.mult)
                ins.then_inc(s_diag, 1)

            def xn_lo(q, c):
                dve.wait_ge(s_xn_hi, DC * q + c + 1)
                lo(act_lo[:, c, tok(q % 2)], xn_tmp[:, c % 2], act_hi[:, c, tok(q % 2)]).then_inc(s_xn, 1)

            def xn(q, c):
                gain = {0: G1, 2: GM, 4: GQ, 6: G2}[q - q % 2]
                if c == 0:
                    dve.wait_ge(s_bc, q + 1)
                if DC * q + c >= 2:
                    dve.wait_ge(s_xn, DC * q + c - 1)
                if q < 2:
                    if q == 0 and c in X_BY_ACT:
                        dve.wait_ge(s_xt_a, X_BY_ACT.index(c) + 1)
                    elif q == 1:
                        dve.wait_ge(s_xt_a, HT + c + 1)
                    else:
                        dve.wait_ge(s_xt, c + 1)
                dve.scalar_tensor_tensor(out=xn_tmp[:, c % 2], in0=xT[:, c, tok(q % 2)],
                                         scalar=gains[:, gain + c:gain + c + 1], in1=ps[:, BC_BANK[q], :],
                                         op0=ALU.mult, op1=ALU.mult).then_inc(s_xn_tmp, 1)
                if c:
                    xn_lo(q, c - 1)
                if c == DC - 1:
                    xn_lo(q, c)

            def first_weights(F_):
                dve.wait_ge(F_.gate_hi, 1)
                lo(gate_lo[:], gate_raw[:], gate_hi[:]).then_inc(F_.gate_lo, 1)
                dve.wait_ge(F_.up_hi, 1)
                lo(up_lo[:], up_raw[:], up_hi[:]).then_inc(F_.up_lo, 1)

            def add(F_, before, k):
                half, d = divmod(k, DC)
                dve.wait_ge(F_.out_done, before + k + 1)
                dve.scalar_tensor_tensor(out=xT[:, d, tok(half)], in0=ps[:, 4 + k % 4, :], scalar=0.5,
                                         in1=xT[:, d, tok(half)], op0=ALU.mult,
                                         op1=ALU.add).then_inc(F_.out_free, 1)

            def ffn(F_):
                def chunk(c, parity, s, first=False, downs=True):
                    dve.wait_ge(F_.gate_hi, c + 2)
                    lo(gate_lo[:], gate_raw[:], gate_hi[:]).then_inc(F_.gate_lo, 1)
                    for half in range(2):
                        dve.wait_ge(F_.up_done, 2 * c + half + 1)
                        dve.wait_ge(F_.silu, 2 * c + half + 1)
                        if not first:
                            dve.wait_ge(F_.h_lo, 2 * c - 1 + half)
                        dve.tensor_tensor(h_sum[:, half], silu[:, half], ps[:, 2 + half, :],
                                          ALU.mult).then_inc(F_.prod, 1)
                        dve.wait_ge(F_.h_hi, 2 * c + half + 1)
                        lo(h_lo[:, 2 * parity + s, tok(half)], h_sum[:, half],
                           h_hi[:, 2 * parity + s, tok(half)]).then_inc(F_.h_lo, 1)
                        if half == 0 and downs:
                            dve.wait_ge(F_.down_hi, c - 1)
                            lo(down_lo[:, s], down_raw[:], down_hi[:, s]).then_inc(F_.down_lo, 1)
                    dve.wait_ge(F_.up_hi, c + 2)
                    lo(up_lo[:], up_raw[:], up_hi[:]).then_inc(F_.up_lo, 1)

                dve.sem_inc(F_.out_free, BANKS)
                chunk(0, 0, 0, first=True, downs=False)
                chunk(1, 0, 1, downs=False)
                with dve.Fori(0, (GROUPS - 1) // 2) as it:
                    for parity in (1, 0):
                        g = 2 * it + (1 if parity else 2)
                        chunk(2 * g, parity, 0)
                        chunk(2 * g + 1, parity, 1)
                        dve.wait_ge(F_.out_free, BANKS + 2 * DC * (g - 1))
                        for k in range(2 * DC):
                            add(F_, 2 * DC * (g - 1), k)

            def row_var(t):
                dve.wait_ge(s_ysq, t + 1)
                dve.tensor_scalar(fstat[:, 1, t:t + 1], fstat[:, 0, t:t + 1], 1.0 / D, EPS, ALU.mult,
                                  ALU.add).then_inc(s_fvar, 1)

            def final_rows(t):
                dve.wait_ge(s_fstd, t + 1)
                newton(fstat[:, 1, t:t + 1], fstat[:, 2, t:t + 1], [fstat[:, i, t:t + 1] for i in (3, 4, 5, 6)],
                       s_fchain, 5 * t)
                if t == 0:
                    dve.wait_ge(s_fin_in, 16)
                if t >= 2:
                    dve.wait_ge(s_out[t % 2], 16 * (t // 2))
                dve.scalar_tensor_tensor(out=y_row[:, t % 2, :],
                                         in0=ps[:, Y_BANK[t]:Y_BANK[t] + 2, :].rearrange("p b n -> p (b n)"),
                                         scalar=fstat[:, 6, t:t + 1], in1=gain_all[:], op0=ALU.mult,
                                         op1=ALU.mult).then_inc(s_y, 1)

            def x_copy(c):
                dve.wait_ge(s_xt_ps, c + 1)
                dve.tensor_copy(xT[:, c, tok(0)], ps[:, c, :]).then_inc(s_xt, 1)

            norm_var(0)
            x_copy(0)
            x_copy(1)
            norm_diag(0)
            x_copy(2)
            x_copy(3)
            dve.wait_ge(f1.gate_hi, 1)
            lo(gate_lo[:], gate_raw[:], gate_hi[:]).then_inc(f1.gate_lo, 1)
            dve.wait_ge(s_gains, 1)
            for c in range(DC):
                xn(0, c)
            norm_var(1)
            norm_diag(1)
            for c in range(DC):
                xn(1, c)
            def a_weight(n):
                dve.wait_ge(a_hi, n + 1)
                lo(wa_lo[:, n % 2], wa_raw[:, n % 2], wa_hi[:, n % 2]).then_inc(a_lo, 1)

            ffn(f1)
            dve.wait_ge(f1.out_free, BANKS + LAST)
            for step in tail_steps(2):
                if step[0] == "add":
                    add(f1, LAST, step[1])
                elif step[0] == "lo":
                    a_weight(step[1])
                elif step[0] == "var":
                    norm_var(step[1])
                elif step[0] == "diag":
                    norm_diag(step[1])
                elif step[0] == "xn":
                    xn(step[1], step[2])

            def pool_lo_part(k):
                g, half = divmod(k, 2)
                dve.wait_ge(s_pl_hi, k + 1)
                lo(pool_lo[:, half], pooled[:, g, tok(half)], pool_hi[:, half]).then_inc(s_pl, 1)

            spills = [0, 0]

            def empty(step):
                if step == ("split", 4):
                    dve.wait_ge(s_wp_hi, 1)
                    lo(wp_lo[:], wp_raw[:], wp_hi[:]).then_inc(s_wp, 1)
                if step[0] == "split":
                    a_weight(step[1])
                elif step[0] == "unit":
                    k = step[1]
                    kind, j, part = a_units[k]
                    bank = ps[:, a_bank[k], :]
                    if k == A_PROJ - 2:
                        pool_lo_part(0)
                        pool_lo_part(1)
                    if kind == "u":
                        dve.wait_ge(a_out, k + 1)
                        if j:
                            dve.wait_ge(s_pooled, j)
                        dve.tensor_copy(u[:, PAD + part * HALF:PAD + (part + 1) * HALF], bank
                                        ).then_inc(a_free, 1)
                    else:
                        dve.wait_ge(a_ehi, a_hi_of[k] + 1)
                    if kind == "pool":
                        to = act_lo[:, DC // 2 + j, tok(part)]
                        dve.scalar_tensor_tensor(out=to, in0=bank, scalar=gains[:, GP + j:GP + j + 1],
                                                 in1=plain(act_hi[:, DC // 2 + j, tok(part)]), op0=ALU.mult,
                                                 op1=ALU.subtract).then_inc(a_free, 1)
                        if k - A_PROJ + 2 < 2 * NG:
                            pool_lo_part(k - A_PROJ + 2)
                    elif kind == "v":
                        c256 = slice((j - 1) * P, (j + 1) * P)
                        lo(v_lo[:, part, c256], bank[:, 0:2 * P], v_hi[:, part, c256]).then_inc(a_free, 1)
                    elif kind in ("q", "k"):
                        slot = a_slot[k]
                        if spills[slot]:
                            dve.wait_ge(s_spill[slot], 32 * spills[slot])
                        lo(stage_lo[:, slot], bank, stage_hi[:, slot]).then_inc(a_free, 1)
                        spills[slot] += 1
                else:
                    g = step[1]
                    w = POOL_WINDOWS[g]
                    sums = (s0, s1)[g % 2]
                    dve.wait_ge(s_wsum, g + 1)
                    dve.wait_ge(a_free, u_done[g])
                    dve.scalar_tensor_tensor(out=pooled[:, g, w:], in0=sums[:, PAD + w:], scalar=1.0 / w,
                                             in1=u[:, PAD + w:], op0=ALU.mult, op1=ALU.subtract)
                    dve.tensor_tensor(head_mean[:, 0:w], sums[:, PAD:PAD + w], recip_count[:, 0:w],
                                      ALU.mult).then_inc(s_dchain, 1)
                    dve.wait_ge(s_dchain, g + 1)
                    dve.tensor_tensor(pooled[:, g, 0:w], head_mean[:, 0:w], u[:, PAD:PAD + w],
                                      ALU.subtract).then_inc(s_pooled, 1)

            for c in range(DC):
                xn(3, c)
                if c == 1:
                    for step in a_empty[:2]:
                        empty(step)
            dve.wait_ge(s_counts, PAD)
            dve.wait_ge(s_pads, 3)
            for step in a_empty[2:]:
                empty(step)

            def b_weight(n):
                dve.wait_ge(b_hi, n + 1)
                lo(wb_lo[:, n % 2], wb_raw[:, n % 2], wb_hi[:, n % 2]).then_inc(b_lo, 1)

            def stick(m):
                n = (tile_at(m)[1] + 1) * P
                r = rest[:, m % 3, 0:n]
                dve.wait_ge(s_mask, 2 * (m + 1))
                dve.tensor_tensor_scan(r[:, ::-1], r[:, ::-1], r[:, ::-1], 1.0, ALU.mult,
                                       ALU.bypass).then_inc(s_scan, 1)
                if n > HALF:
                    dve.wait_ge(s_scan, m + 1)
                    dve.tensor_tensor(beta[:, m % 4, HALF:n - 1], beta[:, m % 4, HALF:n - 1],
                                      rest[:, m % 3, HALF + 1:n], ALU.mult).then_inc(s_a_far, 1)

            for s in range(M + VALUE_LAG):
                if 0 <= s - STICK_LAG < M:
                    stick(s - STICK_LAG)
                if s < TURN_LAG:
                    for k in pool_among[s]:
                        empty(("unit", k))
                m = s - TURN_LAG
                if m == 0:
                    for slot in range(2):
                        dve.wait_ge(s_spill[slot], 32 * (2 * SBW // P))
                if 0 <= m < M:
                    for nth, bank, first, end in turns(m):
                        dve.wait_ge(s_aT_hi, nth + 1)
                        lo(aT_part(aT_lo, m, first, end),
                           ps[:, bank, 0:(end - first) * P].rearrange("p (j t) -> p j t", t=P),
                           aT_part(aT_hi, m, first, end)).then_inc(s_aT, 1)
                if s >= VALUE_LAG and (s - VALUE_LAG) % 2 == 0:
                    w = (s - VALUE_LAG) // 2
                    h, b = pair_at(w)
                    at = (slice(64 * (h % 2), 64 * (h % 2 + 1)), h // 2, slice(b * 2 * P, (b + 1) * 2 * P))
                    dve.wait_ge(s_o_hi, w + 1)
                    lo(act_lo[at], ps[at[0], 7, (w % 2) * 2 * P:(w % 2 + 1) * 2 * P],
                       act_hi[at]).then_inc(s_o_free, 1)
                if s == M + 2:
                    b_weight(0)
                    b_weight(1)

            for step in B_STEPS:
                k = b_first[step]
                if step[0] == "tile":
                    _, kind, j = step
                    if kind in ADDS:
                        half = int(kind[-1])
                        dve.wait_ge(b_out, k + 1)
                        dve.tensor_tensor(xT[:, j, tok(half)], ps[:, 4 + k % 4, :], xT[:, j, tok(half)],
                                          ALU.add).then_inc(b_free, 1)
                    elif kind == "mk":
                        dve.wait_ge(b_ehi, b_hi_of[k] + 1)
                        lo(mk_lo[:, j, :], ps[:, 4 + k % 4, 0:MEM], mk_hi[:, j, :]).then_inc(b_free, 1)
                    elif kind == "mv" and j % 2:
                        for t in range(MC):
                            c256 = slice((j - 1) * P, (j + 1) * P)
                            dve.wait_ge(b_ehi, b_hi_of[k + t] + 1)
                            lo(mv_lo[:, t, c256], ps[:, 4 + (k + t) % 4, 0:2 * P],
                               mv_hi[:, t, c256]).then_inc(b_free, 1)
                    elif kind in ("q0", "q1"):
                        dve.wait_ge(b_ehi, b_hi_of[k] + 1)
                        lo(mq_lo[:, j, :], ps[:, 4 + k % 4, :], mq_hi[:, j, :]).then_inc(b_free, 1)
                    if b_tile[step] + 2 < len(B_TILES):
                        b_weight(b_tile[step] + 2)
                elif step[0] == "mem_rms":
                    dve.wait_ge(s_mem_sq, MC)
                    dve.tensor_scalar(mvar[:, 1, :], mvar[:, 0, :], 1.0 / D, EPS, ALU.mult,
                                      ALU.add).then_inc(s_mem_chain, 1)
                    dve.wait_ge(s_mem_sq, MC + 1)
                    newton(mvar[:, 1, :], mvar[:, 2, :], [mvar[:, i, :] for i in (3, 4, 5, 6)], s_mem_chain, 1)
                    for c in range(MC):
                        dve.tensor_scalar(mem_rows[:, c, :], mem_rows[:, c, :], mvar[:, 6, c:c + 1], None,
                                          ALU.mult).then_inc(s_mem_scaled, 1)
                elif step[0] == "memT":
                    for c in range(DC + 1):
                        if c < DC:
                            dve.wait_ge(s_memT_ps, c + 1)
                            if c >= 2:
                                dve.wait_ge(s_memT, c - 1)
                            dve.tensor_scalar(mem_tmp[:, c % 2], ps[:, c % 4, 0:MEM],
                                              gains[:, GKV + c:GKV + c + 1], None,
                                              ALU.mult).then_inc(s_memT_tmp, 1)
                        if c:
                            dve.wait_ge(s_memT_hi, c)
                            lo(memT_lo[:, c - 1, :], mem_tmp[:, (c - 1) % 2],
                               memT_hi[:, c - 1, :]).then_inc(s_memT, 1)
                elif step[0] == "ffn":
                    first_weights(f2)
                elif step[0] == "tot":
                    norm_var(step[1])
                    norm_diag(step[1])
                elif step[0] == "xn":
                    xn(step[1], step[2])
                elif step[0] == "S":
                    w = step[1] * MHEADS + step[2]
                    st = mstat[:, w % 2]
                    dve.wait_ge(s_S, w + 1)
                    dve.tensor_reduce(st[:, 0, :], ps[:, 0:2, :].rearrange("p b (t m) -> p (b t) m", m=MEM),
                                      AX_X, ALU.max).then_inc(s_mx, 1)
                    dve.wait_ge(s_mx, w + 1)
                    dve.tensor_scalar(st[:, 1, :], st[:, 0, :], -MEM_SCALE, None, ALU.mult).then_inc(s_nmx, 1)
                    dve.wait_ge(s_exp, HT * (w + 1))
                    dve.reciprocal(st[:, 3, :], st[:, 2, :]).then_inc(s_rinv, 1)
                    dve.wait_ge(s_rinv, w + 1)
                    for t in range(HT):
                        ins = dve.tensor_scalar(prob[:, w % 2, t, :], prob[:, w % 2, t, :], st[:, 3, t:t + 1], None,
                                                ALU.mult)
                    ins.then_inc(s_prob, 1)
                elif step[0] == "T":
                    _, half, h = step
                    w = half * MHEADS + h
                    dve.wait_ge(s_pT_hi, w + 1)
                    lo(pT_lo[:].rearrange("p m t -> p (m t)"), ps[:, 2:4, :].rearrange("p m t -> p (m t)"),
                       pT_hi[:].rearrange("p m t -> p (m t)")).then_inc(s_pT, 1)
                elif step[0] == "PV":
                    _, half, h = step
                    for e in range(HD):
                        dve.wait_ge(b_ehi, b_hi_of[k + e] + 1)
                        lo(act_lo[:, HD * h + e, tok(half)], ps[:, 4 + (k + e) % 4, :],
                           act_hi[:, HD * h + e, tok(half)]).then_inc(b_free, 1)
            norm_var(7)
            norm_diag(7)
            for c in range(DC):
                xn(7, c)
            ffn(f2)
            dve.wait_ge(f2.out_free, BANKS + LAST)
            for k in range(2 * DC):
                add(f2, LAST, k)
                if k >= DC + 1 and k % 2:
                    row_var((k - DC) // 2)
                    final_rows((k - DC) // 2)
            for step, t in Y_STEPS:
                if t >= HT and step == "mean":
                    row_var(t)
                elif t >= HT and step == "rows":
                    final_rows(t)


_INS = ["x", "mem", "ffn1_norm", "ffn1_w_gate", "ffn1_w_up", "ffn1_w_down", "mix_norm", "w_in", "w_pool",
        "pool_scale", "w_out", "mem_q_norm", "mem_kv_norm", "mem_w_q", "mem_w_kv", "mem_w_o",
        "ffn2_norm", "ffn2_w_gate", "ffn2_w_up", "ffn2_w_down", "final_norm"]


def kernel(**inputs):
    import numpy as np
    from concourse import bacc
    from concourse.bass_utils import run_bass_kernel_spmd

    nc = bacc.Bacc("TRN2", target_bir_lowering=False, num_devices=1, dynamic_dma_scratch_size=1024)
    arrays, args = {}, []
    for name in _INS:
        a = np.ascontiguousarray(inputs[name])
        arrays[f"in_{name}"] = a
        args.append(nc.dram_tensor(f"in_{name}", a.shape, mybir.dt.from_np(a.dtype), kind="ExternalInput").ap())
    shape = arrays["in_x"].shape
    args.append(nc.dram_tensor("out_y", shape, F32, kind="ExternalOutput").ap())
    layer_program(nc, *args)
    result = run_bass_kernel_spmd(nc, [arrays], core_ids=[0])
    return result.results[0]["out_y"]
```
